# Optimizing a Trainium2 kernel written in Bass

```python
import math
import jax, jax.numpy as jnp
from jax import lax
import numpy as np

D_MODEL = 1024
BATCH = 1
SEQ = 1024
DEPTH = 1
DEC_BATCH = 1
DEC_SEQ = 32
PAST_LEN = 1024

CHUNK = 64
Q_BLOCK = 128
HEAD_DIM = 64
FOX_HEADS = 8
DSA_HEADS = 8
DSA_KV_HEADS = 2
IDX_HEADS = 4
IDX_DIM = 64
IDX_TOPK_MAX = 256
ROPE_THETA = 500000.0
ROT_DIM = HEAD_DIM // 4
FOX_WIDTH = FOX_HEADS * HEAD_DIM
DSA_WIDTH = DSA_HEADS * HEAD_DIM
DSA_KV_WIDTH = DSA_KV_HEADS * HEAD_DIM
MIX_WIDTH = FOX_WIDTH + DSA_WIDTH
D_FF = -(-8 * D_MODEL // (3 * 256)) * 256
ALPHA = (2 * DEPTH) ** 0.25
BETA = (8 * DEPTH) ** -0.25
LN_EPS = 1e-5
FORGET_BIAS_INIT = 3.0
IN_SIZES = (FOX_WIDTH, FOX_WIDTH, FOX_WIDTH, FOX_HEADS,
            DSA_WIDTH, DSA_KV_WIDTH, DSA_KV_WIDTH, IDX_HEADS * IDX_DIM, IDX_DIM, IDX_HEADS)
IN_WIDTH = sum(IN_SIZES)
IN_VALUE_PARTS = (2, 6)

kernel_name = "fox_dsa_hybrid_stream_step"

def layer_norm(x, g, b):
    xf = x.astype(jnp.float32)
    mu = jnp.mean(xf, -1, keepdims=True)
    var = jnp.mean(jnp.square(xf - mu), -1, keepdims=True)
    return ((xf - mu) * lax.rsqrt(var + LN_EPS) * g + b).astype(x.dtype)

def rope_tables(positions):
    half = ROT_DIM // 2
    inv_freq = ROPE_THETA ** (-jnp.arange(half, dtype=jnp.float32) * 2.0 / ROT_DIM)
    ang = positions.astype(jnp.float32)[:, None] * inv_freq[None, :]
    return jnp.cos(ang), jnp.sin(ang)

def partial_rope(x, cos, sin):
    half = ROT_DIM // 2
    x1, x2 = x[..., :half], x[..., half:ROT_DIM]
    cos = cos.astype(x.dtype)
    sin = sin.astype(x.dtype)
    return jnp.concatenate([x1 * cos - x2 * sin, x2 * cos + x1 * sin, x[..., ROT_DIM:]], axis=-1)

def project_inputs(x, positions, w_in, b_forget):
    B, S, _ = x.shape
    points, acc = [], 0
    for size in IN_SIZES[:-1]:
        acc += size
        points.append(acc)
    fq, fk, fv, ff, dq, dk, dv, iq, ik, iw = jnp.split(x @ w_in, points, axis=-1)
    cos, sin = rope_tables(positions)
    c4, s4 = cos[None, :, None, :], sin[None, :, None, :]
    fox_q = fq.reshape(B, S, FOX_HEADS, HEAD_DIM)
    fox_k = fk.reshape(B, S, FOX_HEADS, HEAD_DIM)
    fox_v = fv.reshape(B, S, FOX_HEADS, HEAD_DIM)
    fox_logf = jax.nn.log_sigmoid((ff + b_forget).astype(jnp.float32))
    dsa_q = partial_rope(dq.reshape(B, S, DSA_HEADS, HEAD_DIM), c4, s4)
    dsa_k = partial_rope(dk.reshape(B, S, DSA_KV_HEADS, HEAD_DIM), c4, s4)
    dsa_v = dv.reshape(B, S, DSA_KV_HEADS, HEAD_DIM)
    idx_q = partial_rope(iq.reshape(B, S, IDX_HEADS, IDX_DIM), c4, s4)
    idx_k = partial_rope(ik, cos[None], sin[None])
    return fox_q, fox_k, fox_v, fox_logf, dsa_q, dsa_k, dsa_v, idx_q, idx_k, iw

def fox_prompt(q, k, v, logf):
    B, S, H, Dh = q.shape
    ct = jnp.cumsum(logf, axis=1).transpose(0, 2, 1)
    kpos = jnp.arange(S)
    scale = Dh ** -0.5

    def block(i):
        start = i * Q_BLOCK
        qb = lax.dynamic_slice_in_dim(q, start, Q_BLOCK, axis=1)
        cq = lax.dynamic_slice_in_dim(ct, start, Q_BLOCK, axis=2)
        s = jnp.einsum('bqhd,bshd->bhqs', qb, k).astype(jnp.float32) * scale
        s = s + cq[..., None] - ct[:, :, None, :]
        qpos = start + jnp.arange(Q_BLOCK)
        s = jnp.where(kpos[None, :] <= qpos[:, None], s, -jnp.inf)
        p = jax.nn.softmax(s, axis=-1).astype(v.dtype)
        return jnp.einsum('bhqs,bshd->bqhd', p, v)

    out = lax.map(block, jnp.arange(S // Q_BLOCK))
    return jnp.moveaxis(out, 0, 1).reshape(B, S, H * Dh)

def fox_sample(q, k_new, v_new, lf_new, k_past, v_past, lf_past):
    B, T, H, Dh = q.shape
    P = k_past.shape[1]
    k = jnp.concatenate([k_past, k_new], axis=1)
    v = jnp.concatenate([v_past, v_new], axis=1)
    lp = lf_past.astype(jnp.float32)
    d_past = lax.cumsum(lp, axis=1, reverse=True) - lp
    c_new = jnp.cumsum(lf_new.astype(jnp.float32), axis=1)
    key_bias = jnp.concatenate([d_past, -c_new], axis=1)
    s = jnp.einsum('bqhd,bshd->bhqs', q, k).astype(jnp.float32) * Dh ** -0.5
    s = s + c_new.transpose(0, 2, 1)[..., None] + key_bias.transpose(0, 2, 1)[:, :, None, :]
    kpos = jnp.arange(P + T)
    qpos = P + jnp.arange(T)
    s = jnp.where(kpos[None, :] <= qpos[:, None], s, -jnp.inf)
    p = jax.nn.softmax(s, axis=-1).astype(v.dtype)
    return jnp.einsum('bhqs,bshd->bqhd', p, v).reshape(B, T, H * Dh)

def gathered_attention(q, k, v, idx, valid):
    B, Q, H, Dh = q.shape
    KVH = k.shape[2]
    gather = jax.vmap(lambda t, i: t[i])
    ks = gather(k, idx)
    vs = gather(v, idx)
    qg = q.reshape(B, Q, KVH, H // KVH, Dh)
    s = jnp.einsum('bqhgd,bqnhd->bqhgn', qg, ks).astype(jnp.float32) * Dh ** -0.5
    s = jnp.where(valid[:, :, None, None, :], s, -jnp.inf)
    p = jax.nn.softmax(s, axis=-1).astype(v.dtype)
    return jnp.einsum('bqhgn,bqnhd->bqhgd', p, vs).reshape(B, Q, H * Dh)

def dsa_select_attend(q, iq, iw, q_pos, k, v, ik, k_pos, top_k):
    logits = jnp.einsum('bqhd,bsd->bqhs', iq, ik)
    score = jnp.einsum('bqh,bqhs->bqs', iw, jax.nn.relu(logits)).astype(jnp.float32)
    q_chunk = q_pos // CHUNK
    adm = (k_pos[None, :] // CHUNK) <= q_chunk[:, None]
    score = jnp.where(adm[None], score, -jnp.inf)
    _, idx = lax.top_k(score, top_k)
    valid = (k_pos[idx] // CHUNK) <= q_chunk[None, :, None]
    return gathered_attention(q, k, v, idx, valid)

def dsa_prompt(q, iq, iw, k, v, ik, top_k):
    B, S = q.shape[:2]
    kpos = jnp.arange(S)

    def block(i):
        start = i * Q_BLOCK
        sl = lambda t: lax.dynamic_slice_in_dim(t, start, Q_BLOCK, axis=1)
        return dsa_select_attend(sl(q), sl(iq), sl(iw), start + jnp.arange(Q_BLOCK), k, v, ik, kpos, top_k)

    out = lax.map(block, jnp.arange(S // Q_BLOCK))
    return jnp.moveaxis(out, 0, 1).reshape(B, S, -1)

def post_sublayers(x, mix, ln1_g, ln1_b, w_gate, w_up, w_down, ln2_g, ln2_b):
    h = layer_norm(ALPHA * x + mix, ln1_g, ln1_b)
    f = (jax.nn.silu(h @ w_gate) * (h @ w_up)) @ w_down
    return layer_norm(ALPHA * h + f, ln2_g, ln2_b)

def setup_inputs(seed: int = 0) -> dict:
    key = jax.random.key(seed)
    ks = jax.random.split(key, 20)
    f32 = jnp.float32
    n = lambda k, s: jax.random.normal(k, s, f32)
    x_prompt = n(ks[0], (BATCH, SEQ, D_MODEL))
    x_sample = n(ks[1], (DEC_BATCH, DEC_SEQ, D_MODEL))
    cache_fox_k = n(ks[2], (DEPTH, DEC_BATCH, PAST_LEN, FOX_HEADS, HEAD_DIM))
    cache_fox_v = n(ks[3], (DEPTH, DEC_BATCH, PAST_LEN, FOX_HEADS, HEAD_DIM)) * BETA
    cache_fox_logf = jax.nn.log_sigmoid(FORGET_BIAS_INIT + n(ks[4], (DEPTH, DEC_BATCH, PAST_LEN, FOX_HEADS)))
    cache_dsa_k = n(ks[5], (DEPTH, DEC_BATCH, PAST_LEN, DSA_KV_HEADS, HEAD_DIM))
    cache_dsa_v = n(ks[6], (DEPTH, DEC_BATCH, PAST_LEN, DSA_KV_HEADS, HEAD_DIM)) * BETA
    cache_idx_k = n(ks[7], (DEPTH, DEC_BATCH, PAST_LEN, IDX_DIM))
    col_scale = jnp.concatenate([jnp.full((sz,), BETA if i in IN_VALUE_PARTS else 1.0, f32)
                                 for i, sz in enumerate(IN_SIZES)])
    w_in = n(ks[8], (DEPTH, D_MODEL, IN_WIDTH)) * D_MODEL ** -0.5 * col_scale
    b_forget = FORGET_BIAS_INIT + 0.5 * n(ks[9], (DEPTH, FOX_HEADS))
    w_out = n(ks[10], (DEPTH, MIX_WIDTH, D_MODEL)) * MIX_WIDTH ** -0.5 * BETA
    ln1_g = 1.0 + 0.05 * n(ks[11], (DEPTH, D_MODEL))
    ln1_b = 0.02 * n(ks[12], (DEPTH, D_MODEL))
    w_gate = n(ks[13], (DEPTH, D_MODEL, D_FF)) * D_MODEL ** -0.5
    w_up = n(ks[14], (DEPTH, D_MODEL, D_FF)) * D_MODEL ** -0.5 * BETA
    w_down = n(ks[15], (DEPTH, D_FF, D_MODEL)) * D_FF ** -0.5 * BETA
    ln2_g = 1.0 + 0.05 * n(ks[16], (DEPTH, D_MODEL))
    ln2_b = 0.02 * n(ks[17], (DEPTH, D_MODEL))
    return {"x_prompt": x_prompt, "x_sample": x_sample,
            "cache_fox_k": cache_fox_k, "cache_fox_v": cache_fox_v, "cache_fox_logf": cache_fox_logf,
            "cache_dsa_k": cache_dsa_k, "cache_dsa_v": cache_dsa_v, "cache_idx_k": cache_idx_k,
            "w_in": w_in, "b_forget": b_forget, "w_out": w_out, "ln1_g": ln1_g, "ln1_b": ln1_b,
            "w_gate": w_gate, "w_up": w_up, "w_down": w_down, "ln2_g": ln2_g, "ln2_b": ln2_b}

def reference(x_prompt, x_sample, cache_fox_k, cache_fox_v, cache_fox_logf, cache_dsa_k, cache_dsa_v,
              cache_idx_k, w_in, b_forget, w_out, ln1_g, ln1_b, w_gate, w_up, w_down, ln2_g, ln2_b):
    S = x_prompt.shape[1]
    T = x_sample.shape[1]
    P = cache_fox_k.shape[2]
    topk_prompt = min(IDX_TOPK_MAX, S // 4)
    topk_sample = min(IDX_TOPK_MAX, (P + T) // 4)
    pos_p = jnp.arange(S)
    pos_s = P + jnp.arange(T)
    kpos_s = jnp.arange(P + T)
    yp, ys = x_prompt, x_sample
    p_st = [[] for _ in range(6)]
    s_st = [[] for _ in range(6)]
    for l in range(DEPTH):
        fq, fk, fv, flf, dq, dk, dv, iq, ik, iw = project_inputs(yp, pos_p, w_in[l], b_forget[l])
        fox_o = fox_prompt(fq, fk, fv, flf)
        dsa_o = dsa_prompt(dq, iq, iw, dk, dv, ik, topk_prompt)
        mix = jnp.concatenate([fox_o, dsa_o], axis=-1) @ w_out[l]
        yp = post_sublayers(yp, mix, ln1_g[l], ln1_b[l], w_gate[l], w_up[l], w_down[l], ln2_g[l], ln2_b[l])
        for lst, arr in zip(p_st, (fk, fv, flf, dk, dv, ik)):
            lst.append(arr)
        gq, gk, gv, glf, eq, ek, ev, jq, jk, jw = project_inputs(ys, pos_s, w_in[l], b_forget[l])
        fox_s = fox_sample(gq, gk, gv, glf, cache_fox_k[l], cache_fox_v[l], cache_fox_logf[l])
        k_all = jnp.concatenate([cache_dsa_k[l], ek], axis=1)
        v_all = jnp.concatenate([cache_dsa_v[l], ev], axis=1)
        ik_all = jnp.concatenate([cache_idx_k[l], jk], axis=1)
        dsa_s = dsa_select_attend(eq, jq, jw, pos_s, k_all, v_all, ik_all, kpos_s, topk_sample)
        mix_s = jnp.concatenate([fox_s, dsa_s], axis=-1) @ w_out[l]
        ys = post_sublayers(ys, mix_s, ln1_g[l], ln1_b[l], w_gate[l], w_up[l], w_down[l], ln2_g[l], ln2_b[l])
        for lst, arr in zip(s_st, (gk, gv, glf, ek, ev, jk)):
            lst.append(arr)
    p_fox_k, p_fox_v, p_fox_logf, p_dsa_k, p_dsa_v, p_idx_k = [jnp.stack(a, axis=0) for a in p_st]
    s_fox_k, s_fox_v, s_fox_logf, s_dsa_k, s_dsa_v, s_idx_k = [jnp.stack(a, axis=0) for a in s_st]
    return (yp, ys, p_fox_k, p_fox_v, p_fox_logf, p_dsa_k, p_dsa_v, p_idx_k,
            s_fox_k, s_fox_v, s_fox_logf, s_dsa_k, s_dsa_v, s_idx_k)


_drawn_inputs = setup_inputs


def setup_inputs(seed=0):
    import zlib

    import numpy as np

    out = dict(_drawn_inputs(seed))
    spreads = {}
    factors = {'cache_fox_k': 2.694,
     'cache_fox_logf': 8.0,
     'cache_dsa_k': 3.407,
     'cache_idx_k': 3.069,
     'ln1_b': 2.841,
     'ln2_b': 2.88}
    for name, (base, spread) in spreads.items():
        noise = np.random.default_rng([zlib.crc32(name.encode()), seed]).standard_normal(out[name].shape)
        drawn = base * np.exp(spread * noise) if base else spread * noise
        out[name] = __import__('jax').numpy.asarray(drawn.astype(out[name].dtype))
    for name, factor in factors.items():
        out[name] = (out[name] * factor).astype(out[name].dtype)
    return out
```

```python
import concourse.bass as bass
from concourse import mybir

F32 = mybir.dt.float32
F32R = mybir.dt.float32r
BF16 = mybir.dt.bfloat16
FP16 = mybir.dt.float16
I32 = mybir.dt.int32
I16 = mybir.dt.int16
U16 = mybir.dt.uint16
ALU = mybir.AluOpType
ACT = mybir.ActivationFunctionType

P = 128
D = 1024
KD = D // P
SEQ, NEW, PAST = 1024, 32, 1024
ROWS = SEQ + NEW
NT = SEQ // P
TILES = [(t, t * P, P) for t in range(NT)] + [(NT, SEQ, NEW)]
KEYS_S = PAST + NEW
HD = 64
FOX_H, DSA_H, KV_H, IDX_H = 8, 8, 2, 4
ROT = HD // 4
HALF = ROT // 2
CHUNK = 64
TOPK = 256
D_FF = -(-8 * D // (3 * 256)) * 256
ALPHA = 2.0 ** 0.25
LN_EPS = 1e-5
SCALE = HD ** -0.5
BIG = 1e30
LOWEST = -3e38

C_FQ, C_FK, C_FV = 0, 512, 1024
C_FF = 1536
C_DQ = C_FF + FOX_H
C_DK = C_DQ + DSA_H * HD
C_DV = C_DK + KV_H * HD
C_IQ = C_DV + KV_H * HD
C_IK = C_IQ + IDX_H * HD
C_IW = C_IK + HD
IN_WIDTH = C_IW + IDX_H

TC = ROWS // 3
NCH = 3

SEG = []
_at = 0
for _t in range(TOPK // P, NT):
    SEG.append((_t, _at, P, (_t + 1) * P))
    _at += (_t + 1) * P
SEG.append((NT, _at, NEW, KEYS_S))
SCORES = _at + KEYS_S
NSEG = len(SEG)
SETS = [slice(0, 4), slice(4, NSEG)]


def f32(ap):
    return ap.bitcast(F32)


class Places:

    def __init__(self, nc, start, end):
        self.nc, self.at, self.end = nc, start, end

    def __call__(self, name, shape, dt):
        n = 2 if dt in (BF16, FP16) else 4
        for s in shape[1:]:
            n *= s
        t = self.nc.alloc_sbuf_tensor_at(name, shape, dt, offset=self.at)
        self.at += -(-n // 32) * 32
        assert self.at <= self.end, (name, self.at - self.end)
        return t


def build(nc, d):
    base = -(-nc.sbuf_base // 64) * 64
    end = nc.sbuf_usable_end
    t_size = 2 * 2 * 4 * ROWS * 4
    keep = Places(nc, base, end)
    c = {}
    c["score"] = keep("score", [P, SCORES], F32)
    c["ident"] = keep("ident", [P, P], F32)
    c["ident16"] = keep("ident16", [P, P], BF16)
    c["causal16"] = keep("causal16", [P, P], BF16)
    c["corner"] = keep("corner", [P, 2 * P], F32)
    c["causal_s16"] = keep("causal_s16", [P, NEW], BF16)
    c["logf"] = keep("logf", [P, NT + 1, FOX_H], F32)
    tr = keep.at
    c["t_region"] = tr
    rest = tr + t_size
    c["rest"] = rest
    c["end"] = end
    tp = Places(nc, tr, rest)
    c["kT_hi"] = tp("fox_kT_hi", [P, 4, ROWS], F32R)
    c["kT_lo"] = tp("fox_kT_lo", [P, 4, ROWS], F32R)
    c["qT_hi"] = tp("fox_qT_hi", [P, 4, ROWS], F32R)
    c["qT_lo"] = tp("fox_qT_lo", [P, 4, ROWS], F32R)
    rp = Places(nc, rest, end)
    c["mix"] = rp("mix", [P, NT + 1, D], F32)
    c["after_mix"] = rp.at
    project(nc, d, c)
    fox(nc, d, c)
    dsa(nc, d, c)
    mix_out(nc, d, c)
    ffn(nc, d, c)



IX = (IDX_H + 1) * HD

GROUPS = [("ix", [(C_IQ, IX + IDX_H), (C_FF, FOX_H)], False),
          ("dq", [(C_DQ, 256)], False), ("fv", [(C_FV, 256)], False),
          ("dq", [(C_DQ + 256, 256)], False), ("fv", [(C_FV + 256, 256)], False),
          ("dkv", [(C_DK, 256)], False),
          ("fk", [(C_FK, 256)], True), ("fk", [(C_FK + 256, 256)], True),
          ("fq", [(C_FQ, 256)], True), ("fq", [(C_FQ + 256, 256)], True)]
NG = len(GROUPS)
FK = [g[0] for g in GROUPS].index("fk")
IX_GAP = 3


def width(g):
    return sum(n for _, n in GROUPS[g][1])


UNITS = []
for _g, (_name, _, _tr) in enumerate(GROUPS):
    if _tr:
        UNITS += [(_g, _m, _c) for _m in range(2) for _c in range(NCH)]
    else:
        UNITS += [(_g, _t, None) for _t in range(NT + 1)]
OF_GROUP = [[u for u, x in enumerate(UNITS) if x[0] == g] for g in range(NG)]
ROPED = [u for u, x in enumerate(UNITS) if GROUPS[x[0]][0] in ("ix", "dq", "dkv")]
STAGED = [u for u, x in enumerate(UNITS) if GROUPS[x[0]][0] in ("dq", "dkv", "fv")]
TRANS = [u for u, x in enumerate(UNITS) if GROUPS[x[0]][2]]
NSTAGE = 3


def project(nc, d, c):
    from contextlib import ExitStack
    with ExitStack() as ctx:
        def sem(name):
            return ctx.enter_context(nc.semaphore(name))

        tr, rest, end = c["t_region"], c["rest"], c["end"]
        pl = Places(nc, rest, end)
        x_hi = pl("x_hi", [P, KD, ROWS], F32R)
        x_lo = pl("x_lo", [P, KD, ROWS], F32R)
        w_hi = [pl(f"w_hi{s}", [P, KD, 256], F32R) for s in range(2)]
        w_lo = [pl(f"w_lo{s}", [P, KD, 256], F32R) for s in range(2)]
        w_raw = pl("w_raw", [P, KD, 256], F32)
        half = tr + (rest - tr) // 2
        a = Places(nc, tr, half)
        x_raw = a("x_raw", [P, KD, ROWS], F32)
        a = Places(nc, tr, half)
        ix_row = a("ix_row", [P, NT + 1, IX + HD], F32)
        relu = [a(f"relu{s}", [P, KEYS_S], F32) for s in range(2)]
        past_ik = a("past_ik", [P, PAST], F32)
        b = Places(nc, half, rest)
        iT_hi = b("iT_hi", [P, 3, ROWS], F32R)
        iT_lo = b("iT_lo", [P, 3, ROWS], F32R)
        iT_new = b("iT_new", [P, 3, NEW], F32)
        b = Places(nc, half, rest)
        w0_raw = b("w0_raw", [P, KD, width(0)], F32)
        w0_hi = b("w0_hi", [P, KD, width(0)], F32R)
        w0_lo = b("w0_lo", [P, KD, width(0)], F32R)
        stage = [pl(f"stage{s}", [P, 256], F32) for s in range(NSTAGE)]
        tstage = [pl(f"tstage{s}", [P, TC], F32) for s in range(2)]
        iwff = pl("iwff", [P, NT + 1, IDX_H + FOX_H], F32)
        zf = pl("zf", [P, NT + 1, FOX_H], F32)
        az = pl("az", [P, NT + 1, FOX_H], F32)
        lz = pl("lz", [P, NT + 1, FOX_H], F32)
        bf = pl("b_forget_rows", [P, FOX_H], F32)
        cos = pl("cos", [P, NT + 1, HALF], F32)
        sin = pl("sin", [P, NT + 1, HALF], F32)
        ra = pl("rope_a", [P, IDX_H + 1, HALF], F32)
        rb = pl("rope_b", [P, IDX_H + 1, HALF], F32)
        rc = pl("rope_c", [P, IDX_H + 1, HALF], F32)
        rd = pl("rope_d", [P, IDX_H + 1, HALF], F32)
        key_buf = pl("key_buf", [P, KEYS_S], I32)
        cnt = pl("cnt", [P, NSEG], F32)
        want = pl("want", [P, NSEG], F32)
        reached = pl("reached", [P, NSEG], F32)
        low = pl("low", [P, NSEG], F32)
        candidate = pl("candidate", [P, NSEG], F32)
        top_key = pl("top_key", [P, NSEG], F32)
        bit = pl("bit", [P, 2], F32)
        score, ident = c["score"], c["ident"]

        pj = ctx.enter_context(nc.psum_tensor("pj", [P, 2, 512], F32))
        pi = ctx.enter_context(nc.psum_tensor("pi", [P, 6 * 512], F32))

        x_loaded = [sem(f"x_loaded{k}") for k in range(KD)]
        x_hi_done, x_lo_done = sem("x_hi_done"), sem("x_lo_done")
        w0_loaded, w_loaded, w_hi_done, w_lo_done = sem("w0_loaded"), sem("w_loaded"), sem("w_hi_done"), sem("w_lo_done")
        unit_done, unit_out = sem("unit_done"), sem("unit_out")
        roped = sem("roped")
        t_lo_done = sem("t_lo_done")
        stage_free = [sem(f"stage_free{s}") for s in range(NSTAGE)]
        tstage_free = [sem(f"tstage_free{s}") for s in range(2)]
        small_loaded, past_loaded = sem("small_loaded"), sem("past_loaded")
        consts, rope_step = sem("consts"), sem("rope_step")
        i_tr, i_hi, i_lo, i_new = sem("i_tr"), sem("i_hi"), sem("i_lo"), sem("i_new")
        i_qk, i_relu, i_sum = sem("i_qk"), sem("i_relu"), sem("i_sum")
        z_done, l_done, logf_done = sem("z_done"), sem("l_done"), sem("logf_done")
        step = sem("step")
        key_done, planes_done = sem("key_done"), sem("planes_done")
        bank_step = sem("rows_out")
        block = ctx.enter_context(nc.Block())

        x_rows = d["xT"].rearrange("(k p) n -> k p n", p=P)
        w_cols = d["w_in"].rearrange("(k p) n -> p k n", p=P)

        def weights(g):
            return (w0_raw, w0_hi, w0_lo) if g == 0 else (w_raw, w_hi[g % 2], w_lo[g % 2])

        def hi_plane(j):
            _, at, rows, L = SEG[j]
            return score[0:rows, at:at + L].bitcast(I16)[:, 0:L]

        def lo_plane(j):
            _, at, rows, L = SEG[j]
            return score[0:rows, at:at + L].bitcast(U16)[:, L:2 * L]

        def flags(j):
            at = (j % 2) * KEYS_S
            return key_buf[0:SEG[j][2], :].bitcast(BF16)[:, at:at + SEG[j][3]]

        def ranks(j):
            return pi[0:SEG[j][2], 1536 * (j % 2):1536 * (j % 2) + SEG[j][3]]

        def loads_of(g):
            return 16 * sum(len(GROUPS[i][1]) for i in range(1, g + 1))

        def stage_value(i):
            return sum(32 if GROUPS[UNITS[STAGED[j]][0]][0] == "dkv" else 16
                       for j in range(i % NSTAGE, i + 1, NSTAGE))

        IDX = [(j, h) for j in range(NSEG) for h in range(IDX_H)]

        @block.sync
        def _(sp):
            def load_w(g):
                if g >= 2:
                    sp.wait_ge(w_hi_done, g)
                    sp.wait_ge(w_lo_done, g)
                at = 0
                for c0, n in GROUPS[g][1]:
                    sp.dma_start(weights(g)[0][:, :, at:at + n], w_cols[:, :, c0:c0 + n])\
                        .then_inc(w0_loaded if g == 0 else w_loaded, 16)
                    at += n

            load_w(0)
            for k in range(KD):
                sp.dma_start(x_raw[:, k, :], x_rows[k]).then_inc(x_loaded[k], 16)
            sp.dma_start(cos[:, :, :], d["cos"]).then_inc(small_loaded, 16)
            sp.dma_start(sin[:, :, :], d["sin"]).then_inc(small_loaded, 16)
            sp.dma_start(bf[:, :], d["b_forget"].partition_broadcast(P)).then_inc(small_loaded, 16)
            load_w(1)
            sp.wait_ge(x_lo_done, KD)
            for r in range(2):
                sp.dma_start(past_ik[r * HD:(r + 1) * HD, :], d["past_ikT"]).then_inc(past_loaded, 16)
            n_out = 0
            for g in range(NG):
                name = GROUPS[g][0]
                if g >= 1 and g + 1 < NG:
                    load_w(g + 1)
                for u in OF_GROUP[g]:
                    _, t, ch = UNITS[u]
                    if GROUPS[g][2]:
                        i = TRANS.index(u)
                        if name == "fk":
                            sp.wait_ge(unit_out, u + 1)
                            f0 = (g - FK) * 256 + t * P
                            sp.dma_start(d["fkT"][f0:f0 + P, ch * TC:(ch + 1) * TC],
                                         tstage[i % 2][:, :]).then_inc(tstage_free[i % 2], 16)
                        continue
                    _, r0, rows = TILES[t]
                    if u in ROPED:
                        sp.wait_ge(roped, ROPED.index(u) + 1)
                    else:
                        sp.wait_ge(unit_out, u + 1)
                    if name == "ix":
                        sp.dma_start(d["ik"][r0:r0 + rows, :], ix_row[0:rows, t, IX - HD:IX]).then_inc(bank_step, 16)
                        n_out += 16
                    if u not in STAGED:
                        continue
                    i = STAGED.index(u)
                    s = stage[i % NSTAGE]
                    if name == "dkv":
                        sp.dma_start(d["dk"][r0:r0 + rows, :], s[0:rows, 0:P]).then_inc(stage_free[i % NSTAGE], 16)
                        sp.dma_start(d["dv"][r0:r0 + rows, :], s[0:rows, P:2 * P]).then_inc(stage_free[i % NSTAGE], 16)
                    else:
                        c0 = GROUPS[g][1][0][0] - (C_DQ if name == "dq" else C_FV)
                        sp.dma_start(d[name][r0:r0 + rows, c0:c0 + 256], s[0:rows, :]).then_inc(stage_free[i % NSTAGE], 16)
                if g == 2:
                    sp.wait_ge(logf_done, 1)
                    sp.dma_start(d["logf"][0:SEQ, :].rearrange("(t p) h -> p t h", p=P),
                                 c["logf"][:, 0:NT, :]).then_inc(bank_step, 16)
                    sp.dma_start(d["logf"][SEQ:ROWS, :], c["logf"][0:NEW, NT, :]).then_inc(bank_step, 16)
                    n_out += 32
            sp.wait_ge(bank_step, n_out)
            for s in range(NSTAGE):
                last = max(i for i in range(len(STAGED)) if i % NSTAGE == s)
                sp.wait_ge(stage_free[s], stage_value(last))
            nk = len(OF_GROUP[FK]) + len(OF_GROUP[FK + 1])
            for s in range(2):
                sp.wait_ge(tstage_free[s], 16 * (nk // 2))

        @block.scalar
        def _(act):
            def split_w(g):
                n = width(g)
                if g == 0:
                    act.wait_ge(w0_loaded, 16 * len(GROUPS[0][1]))
                else:
                    act.wait_ge(w_loaded, loads_of(g))
                if g >= 3:
                    act.wait_ge(unit_done, OF_GROUP[g - 2][-1] + 1)
                raw, hi, _ = weights(g)
                nc.scalar.copy(hi[:, :, 0:n], raw[:, :, 0:n]).then_inc(w_hi_done, 1)

            def copy_out(u):
                g, t, ch = UNITS[u]
                name = GROUPS[g][0]
                act.wait_ge(unit_done, u + 1)
                if GROUPS[g][2]:
                    i = TRANS.index(u)
                    if i == 0:
                        act.wait_ge(i_sum, len(IDX))
                    if i >= 2:
                        act.wait_ge(t_lo_done, i - 1)
                        if i - 2 < 12:
                            act.wait_ge(tstage_free[i % 2], 16 * ((i - 2) // 2 + 1))
                    hi = c["kT_hi"] if name == "fk" else c["qT_hi"]
                    m = 2 * ((g - FK) % 2) + t
                    sc = 1.0 if name == "fk" else SCALE
                    nc.scalar.activation(tstage[i % 2][:, :], pj[:, u % 2, 0:TC], ACT.Copy, scale=sc)
                    nc.scalar.activation(hi[:, m, ch * TC:(ch + 1) * TC], pj[:, u % 2, 0:TC], ACT.Copy,
                                         scale=sc).then_inc(unit_out, 1)
                    return
                rows = TILES[t][2]
                if name == "ix":
                    if t == 0:
                        act.wait_ge(consts, 5)
                    nc.scalar.copy(iwff[0:rows, t, :], pj[0:rows, u % 2, IX:IX + IDX_H + FOX_H])
                    dst, n = ix_row[0:rows, t, 0:IX], IX
                else:
                    i = STAGED.index(u)
                    if i >= NSTAGE:
                        act.wait_ge(stage_free[i % NSTAGE], stage_value(i - NSTAGE))
                    dst, n = stage[i % NSTAGE][0:rows, :], 256
                nc.scalar.copy(dst, pj[0:rows, u % 2, 0:n]).then_inc(unit_out, 1)

            def index_hi():
                for t, r0, rows in TILES:
                    act.wait_ge(i_tr, t + 1)
                    src = pi[:, (t % 6) * 512:(t % 6) * 512 + 3 * P].rearrange("p (a r) -> p a r", a=3)
                    nc.scalar.copy(iT_hi[:, :, r0:r0 + rows], src[:, :, 0:rows]).then_inc(i_hi, 1)

            def planes(j):
                rows, L = SEG[j][2:]
                act.wait_ge(key_done, j + 1)
                halves = key_buf[0:rows, 0:L]
                nc.scalar.copy(hi_plane(j), halves.bitcast(I16)[:, 1:2 * L:2])
                nc.scalar.copy(lo_plane(j), halves.bitcast(U16)[:, 0:2 * L:2]).then_inc(planes_done, 1)

            def index_relu():
                act.wait_ge(z_done, 1)
                nc.scalar.activation(az[:, :, :], az[:, :, :], ACT.Exp, scale=-1.0).then_inc(l_done, 1)
                act.wait_ge(l_done, 1)
                nc.scalar.activation(lz[:, :, :], az[:, :, :], ACT.Ln, bias=1.0).then_inc(l_done, 1)
                for n, (j, h) in enumerate(IDX):
                    _, _, rows, L = SEG[j]
                    act.wait_ge(i_qk, n + 1)
                    if n >= 2:
                        act.wait_ge(i_sum, n - 1)
                    o = 1536 * (n % 2)
                    nc.scalar.activation(relu[n % 2][0:rows, 0:L], pi[0:rows, o:o + L], ACT.Relu)\
                        .then_inc(i_relu, 1)
                    if h == 1 and j >= 1:
                        planes(j - 1)
                planes(NSEG - 1)

            split_w(0)
            for k in range(KD):
                act.wait_ge(x_loaded[k], 16)
                nc.scalar.copy(x_hi[:, k, :], x_raw[:, k, :]).then_inc(x_hi_done, 1)
            split_w(1)
            act.wait_ge(x_lo_done, KD)
            for g in range(NG):
                if 1 <= g < NG - 1:
                    split_w(g + 1)
                for i, u in enumerate(OF_GROUP[g]):
                    copy_out(u)
                    if g == 1 and i == IX_GAP - 1:
                        index_hi()
                        index_relu()

        @block.gpsimd
        def _(pool):
            ident16, causal16, corner = c["ident16"], c["causal16"], c["corner"]
            nc.gpsimd.memset(ident[:, :], 0.0).then_inc(rope_step, 1)
            nc.gpsimd.memset(causal16[:, :], 0.0).then_inc(rope_step, 1)
            pool.wait_ge(rope_step, 2)
            nc.gpsimd.affine_select(out=ident[:, :], in_=ident[:, :], compare_op=ALU.not_equal, fill=1.0,
                                    base=0, pattern=[[-1, P]], channel_multiplier=1).then_inc(consts, 1)
            nc.gpsimd.affine_select(out=causal16[:, :], in_=causal16[:, :], compare_op=ALU.is_ge, fill=-BIG,
                                    base=0, pattern=[[-1, P]], channel_multiplier=1).then_inc(consts, 1)
            pool.wait_ge(consts, 2)
            nc.gpsimd.tensor_copy(ident16[:, :], ident[:, :]).then_inc(consts, 1)
            nc.gpsimd.memset(corner[:, :], 0.0).then_inc(rope_step, 1)
            nc.gpsimd.memset(iwff[:, :, :], 0.0).then_inc(consts, 1)
            pool.wait_ge(rope_step, 3)
            nc.gpsimd.memset(corner[0:CHUNK, 2 * P - CHUNK:2 * P], -BIG).then_inc(consts, 1)
            steps = [3]

            def split_w(g):
                n = width(g)
                pool.wait_ge(w_hi_done, g + 1)
                raw, hi, lo = weights(g)
                nc.gpsimd.tensor_tensor(lo[:, :, 0:n], raw[:, :, 0:n], f32(hi[:, :, 0:n]), ALU.subtract)\
                    .then_inc(w_lo_done, 1)

            def rope(view, t, rows, heads):
                x1, x2 = view[:, :, 0:HALF], view[:, :, HALF:ROT]
                co = cos[0:rows, t, :].unsqueeze(1).broadcast_to((rows, heads, HALF))
                si = sin[0:rows, t, :].unsqueeze(1).broadcast_to((rows, heads, HALF))
                for out, x, y in ((ra, x1, co), (rb, x2, si), (rc, x2, co), (rd, x1, si)):
                    nc.gpsimd.tensor_tensor(out[0:rows, 0:heads, :], x, y, ALU.mult).then_inc(rope_step, 1)
                steps[0] += 4
                pool.wait_ge(rope_step, steps[0])
                nc.gpsimd.tensor_tensor(x1, ra[0:rows, 0:heads, :], rb[0:rows, 0:heads, :], ALU.subtract)\
                    .then_inc(rope_step, 1)
                steps[0] += 1
                return nc.gpsimd.tensor_tensor(x2, rc[0:rows, 0:heads, :], rd[0:rows, 0:heads, :], ALU.add)

            split_w(1)
            pool.wait_ge(small_loaded, 48)
            for g in range(NG):
                if 1 <= g < NG - 1:
                    split_w(g + 1)
                name = GROUPS[g][0]
                for u in OF_GROUP[g]:
                    _, t, ch = UNITS[u]
                    if GROUPS[g][2]:
                        i = TRANS.index(u)
                        pool.wait_ge(unit_out, u + 1)
                        hi, lo = (c["kT_hi"], c["kT_lo"]) if name == "fk" else (c["qT_hi"], c["qT_lo"])
                        m = 2 * ((g - FK) % 2) + t
                        nc.gpsimd.tensor_tensor(lo[:, m, ch * TC:(ch + 1) * TC], tstage[i % 2][:, :],
                                                f32(hi[:, m, ch * TC:(ch + 1) * TC]), ALU.subtract)\
                            .then_inc(t_lo_done, 1)
                        continue
                    if u not in ROPED:
                        continue
                    rows = TILES[t][2]
                    pool.wait_ge(unit_out, u + 1)
                    if name == "ix":
                        view, heads = ix_row[0:rows, t, 0:IX].rearrange("p (h e) -> p h e", e=HD), IDX_H + 1
                    elif name == "dq":
                        view = stage[STAGED.index(u) % NSTAGE][0:rows, :].rearrange("p (h e) -> p h e", e=HD)
                        heads = 4
                    else:
                        view = stage[STAGED.index(u) % NSTAGE][0:rows, 0:P].rearrange("p (h e) -> p h e", e=HD)
                        heads = KV_H
                    last = rope(view, t, rows, heads)
                    if name == "ix":
                        last.then_inc(rope_step, 1)
                        steps[0] += 1
                        pool.wait_ge(rope_step, steps[0])
                        last = nc.gpsimd.tensor_copy(ix_row[0:rows, t, IX:IX + HD], ix_row[0:rows, t, IX - HD:IX])
                    last.then_inc(roped, 1)
                    pool.wait_ge(rope_step, steps[0])
                    pool.wait_ge(roped, ROPED.index(u) + 1)

        @block.tensor
        def _(pe):
            def units(g, which):
                n = width(g)
                pe.wait_ge(w_lo_done, g + 1)
                _, hi, lo = weights(g)
                for u in OF_GROUP[g][which]:
                    _, t, ch = UNITS[u]
                    if u >= 2:
                        pe.wait_ge(unit_out, u - 1)
                    for k in range(KD):
                        if u == 0:
                            pe.wait_ge(x_lo_done, k + 1)
                        if GROUPS[g][2]:
                            out = pj[:, u % 2, 0:TC]
                            cols, rows = slice(t * P, (t + 1) * P), slice(ch * TC, (ch + 1) * TC)
                            pairs = [(hi[:, k, cols], x_hi[:, k, rows]), (hi[:, k, cols], x_lo[:, k, rows]),
                                     (lo[:, k, cols], x_hi[:, k, rows])]
                        else:
                            _, r0, nr = TILES[t]
                            out = pj[0:nr, u % 2, 0:n]
                            xh, xl = x_hi[:, k, r0:r0 + nr], x_lo[:, k, r0:r0 + nr]
                            pairs = [(xh, hi[:, k, 0:n]), (xh, lo[:, k, 0:n]), (xl, hi[:, k, 0:n])]
                        for i, (l, r) in enumerate(pairs):
                            mm = nc.tensor.matmul(out, l, r, start=(k == 0 and i == 0),
                                                  stop=(k == KD - 1 and i == 2))
                    mm.then_inc(unit_done, 1)

            def index_transposes():
                pe.wait_ge(consts, 5)
                for t, r0, rows in TILES:
                    pe.wait_ge(roped, t + 1)
                    if t >= 6:
                        pe.wait_ge(i_lo, t - 5)
                    o = (t % 6) * 512
                    for a_ in range(3):
                        mm = nc.tensor.transpose(pi[:, o + a_ * P:o + a_ * P + rows],
                                                 ix_row[0:rows, t, a_ * P:(a_ + 1) * P], ident[0:rows, 0:rows])
                    mm.then_inc(i_tr, 1)

            def index_scores():
                pe.wait_ge(i_lo, NT + 1)
                pe.wait_ge(i_new, 1)
                pe.wait_ge(past_loaded, 32)
                for n, (j, h) in enumerate(IDX):
                    t, _, rows, L = SEG[j]
                    if n >= 2:
                        pe.wait_ge(i_relu, n - 1)
                    o = 1536 * (n % 2)
                    part, q = slice(HD * (h % 2), HD * (h % 2) + HD), h // 2
                    if t < NT:
                        qs = slice(t * P, t * P + P)
                        for k0 in range(0, L, 512):
                            ks = slice(k0, min(L, k0 + 512))
                            out = pi[:, o + ks.start:o + ks.stop]
                            nc.tensor.matmul(out, iT_hi[part, q, qs], iT_hi[part, 2, ks], start=True, stop=False)
                            nc.tensor.matmul(out, iT_hi[part, q, qs], iT_lo[part, 2, ks], start=False, stop=False)
                            mm = nc.tensor.matmul(out, iT_lo[part, q, qs], iT_hi[part, 2, ks], start=False, stop=True)
                    else:
                        for k0 in range(0, PAST, 512):
                            nc.tensor.matmul(pi[0:NEW, o + k0:o + k0 + 512], iT_new[part, q, :],
                                             past_ik[part, k0:k0 + 512], start=True, stop=True)
                        mm = nc.tensor.matmul(pi[0:NEW, o + PAST:o + KEYS_S], iT_new[part, q, :],
                                              iT_new[part, 2, :], start=True, stop=True)
                    mm.then_inc(i_qk, 1)

            units(0, slice(None))
            units(1, slice(0, IX_GAP))
            index_transposes()
            index_scores()
            units(1, slice(IX_GAP, None))
            for g in range(2, NG):
                units(g, slice(None))

        @block.vector
        def _(dve):
            def key_of(j):
                t, at, rows, L = SEG[j]
                bits, k = score[0:rows, at:at + L].bitcast(I32), key_buf[0:rows, 0:L]
                if j >= 1:
                    dve.wait_ge(planes_done, j)
                did(nc.vector.tensor_scalar(k, bits, 31, 2 ** 31 - 1, ALU.arith_shift_right, ALU.bitwise_and))
                settled()
                nc.vector.tensor_tensor(k, k, bits, ALU.bitwise_xor).then_inc(key_done, 1)

            n = [0]

            def did(ins):
                n[0] += 1
                ins.then_inc(step, 1)

            def settled():
                dve.wait_ge(step, n[0])

            dve.wait_ge(w_hi_done, 1)
            nc.vector.tensor_tensor(w0_lo[:, :, :], w0_raw[:, :, :], f32(w0_hi[:, :, :]), ALU.subtract)\
                .then_inc(w_lo_done, 1)
            for k in range(KD):
                dve.wait_ge(x_hi_done, k + 1)
                nc.vector.tensor_tensor(x_lo[:, k, :], x_raw[:, k, :], f32(x_hi[:, k, :]), ALU.subtract)\
                    .then_inc(x_lo_done, 1)
            did(nc.vector.memset(cnt[:, :], 0.0))
            did(nc.vector.memset(want[:, :], float(TOPK)))
            dve.wait_ge(consts, 2)
            for j in range(4):
                did(nc.vector.tensor_copy(c["causal_s16"][j * NEW:(j + 1) * NEW, :], c["causal16"][0:NEW, 0:NEW]))
            dve.wait_ge(small_loaded, 48)
            dve.wait_ge(unit_out, OF_GROUP[0][-1] + 1)
            did(nc.vector.tensor_tensor(zf[:, :, :], iwff[:, :, IDX_H:IDX_H + FOX_H],
                                        bf[:, :].unsqueeze(1).broadcast_to((P, NT + 1, FOX_H)), ALU.add))
            settled()
            nc.vector.scalar_tensor_tensor(az[:, :, :], zf[:, :, :], -1.0, zf[:, :, :], ALU.mult, ALU.max)\
                .then_inc(z_done, 1)
            for t, r0, rows in TILES:
                dve.wait_ge(i_hi, t + 1)
                src = pi[:, (t % 6) * 512:(t % 6) * 512 + 3 * P].rearrange("p (a r) -> p a r", a=3)
                nc.vector.tensor_tensor(iT_lo[:, :, r0:r0 + rows], src[:, :, 0:rows],
                                        f32(iT_hi[:, :, r0:r0 + rows]), ALU.subtract).then_inc(i_lo, 1)
            dve.wait_ge(i_lo, NT + 1)
            nc.vector.tensor_tensor(iT_new[:, :, :], f32(iT_hi[:, :, SEQ:ROWS]), f32(iT_lo[:, :, SEQ:ROWS]),
                                    ALU.add).then_inc(i_new, 1)
            dve.wait_ge(l_done, 2)
            nc.vector.scalar_tensor_tensor(c["logf"][:, :, :], zf[:, :, :], 0.0, lz[:, :, :], ALU.min,
                                           ALU.subtract).then_inc(logf_done, 1)
            for i, (j, h) in enumerate(IDX):
                t, at, rows, L = SEG[j]
                dve.wait_ge(i_relu, i + 1)
                w = iwff[0:rows, t, h:h + 1]
                out, r = score[0:rows, at:at + L], relu[i % 2][0:rows, 0:L]
                if h == 0:
                    nc.vector.tensor_scalar(out, r, w, 0.0, ALU.mult, ALU.add).then_inc(i_sum, 1)
                    continue
                dve.wait_ge(i_sum, i)
                nc.vector.scalar_tensor_tensor(out, r, w, out, ALU.mult, ALU.add).then_inc(i_sum, 1)
                if h == IDX_H - 1:
                    dve.wait_ge(i_sum, i + 1)
                    if t < NT:
                        did(nc.vector.memset(score[0:CHUNK, at + L - CHUNK:at + L], LOWEST))
                        settled()
                    key_of(j)

            rel = [0]

            def one(ins):
                rel[0] += 1
                ins.then_inc(step, 1)

            def number(op, plane, j, limit):
                return nc.vector.tensor_scalar(flags(j), plane(j), limit[0:SEG[j][2], j:j + 1], 0.0, op, ALU.add,
                                               accum_out=cnt[0:SEG[j][2], j:j + 1])

            def count(base, plane, j):
                dve.wait_ge(step, base + rel[0] - (0 if j == 0 else 1))
                one(number(ALU.is_ge, plane, j, candidate))

            def next_candidate(base, part, s):
                cols, b = SETS[part], bit[:, part:part + 1]
                dve.wait_ge(step, base + rel[0] - 1)
                if s == 0:
                    one(nc.vector.tensor_tensor(reached[:, cols], cnt[:, cols], want[:, cols], ALU.is_ge))
                elif s == 1:
                    one(nc.vector.scalar_tensor_tensor(low[:, cols], reached[:, cols], b, low[:, cols],
                                                       ALU.mult, ALU.add))
                    one(nc.vector.tensor_scalar(b, b, 0.5, None, ALU.mult))
                else:
                    one(nc.vector.tensor_scalar(candidate[:, cols], low[:, cols], b, None, ALU.add))

            def phase(base, plane, part):
                for i, j in enumerate(range(NSEG)[SETS[part]]):
                    count(base, plane, j)
                    if i < 3:
                        next_candidate(base, 1 - part, i)

            def search(plane, lowest):
                settled()
                did(nc.vector.memset(low[:, :], lowest))
                did(nc.vector.memset(candidate[:, :], lowest + 2.0 ** 15))
                did(nc.vector.memset(bit[:, :], 2.0 ** 15))
                settled()
                for j in range(NSEG)[SETS[0]]:
                    if j >= 2:
                        dve.wait_ge(step, n[0] - 1)
                    did(number(ALU.is_ge, plane, j, candidate))
                per, start = NSEG + 8, n[0]
                with dve.Fori(0, 15) as it:
                    rel[0] = 0
                    phase(it * per + start, plane, 1)
                    phase(it * per + start, plane, 0)
                    assert rel[0] == per
                n[0] = start + 15 * per
                rel[0] = 0
                phase(n[0], plane, 1)
                n[0] += rel[0]
                settled()
                cols = SETS[1]
                did(nc.vector.tensor_tensor(reached[:, cols], cnt[:, cols], want[:, cols], ALU.is_ge))
                settled()
                did(nc.vector.tensor_tensor(low[:, cols], reached[:, cols], low[:, cols], ALU.add))
                settled()

            def still_wanted(plane, limit):
                for j in range(NSEG):
                    if j >= 2:
                        dve.wait_ge(step, n[0] - 1)
                    did(number(ALU.is_gt, plane, j, limit))
                settled()
                did(nc.vector.tensor_tensor(want[:, :], want[:, :], cnt[:, :], ALU.subtract))

            dve.wait_ge(planes_done, NSEG)
            search(hi_plane, -2.0 ** 15)
            did(nc.vector.tensor_copy(top_key[:, :], low[:, :]))
            settled()
            still_wanted(hi_plane, top_key)
            for j in range(NSEG):
                did(nc.vector.scalar_tensor_tensor(lo_plane(j), hi_plane(j), top_key[0:SEG[j][2], j:j + 1],
                                                   lo_plane(j), ALU.is_equal, ALU.mult))
            search(lo_plane, 0.0)
            still_wanted(lo_plane, low)
            settled()
            for j0 in range(0, NSEG, 2):
                pair = range(j0, min(NSEG, j0 + 2))
                for s in range(7):
                    for i, j in enumerate(pair):
                        rows = SEG[j][2]
                        e, r = flags(j), ranks(j)
                        top, lo, w = (x[0:rows, j:j + 1] for x in (top_key, low, want))
                        if s == 0:
                            if j >= 2:
                                dve.wait_ge(step, n[0] - i)
                            did(nc.vector.tensor_scalar(e, lo_plane(j), lo, None, ALU.is_equal))
                            continue
                        dve.wait_ge(step, n[0] - (len(pair) - 1))
                        if s == 1:
                            did(nc.vector.scalar_tensor_tensor(e, hi_plane(j), top, e, ALU.is_equal, ALU.mult))
                        elif s == 2:
                            did(nc.vector.tensor_tensor_scan(r, e, e, 0.0, ALU.add, ALU.bypass))
                        elif s == 3:
                            did(nc.vector.scalar_tensor_tensor(e, r, w, e, ALU.is_le, ALU.mult))
                        elif s == 4:
                            did(nc.vector.scalar_tensor_tensor(e, lo_plane(j), lo, e, ALU.is_gt, ALU.add))
                        elif s == 5:
                            did(nc.vector.scalar_tensor_tensor(e, hi_plane(j), top, e, ALU.is_gt, ALU.add))
                        else:
                            _, at, rows, L = SEG[j]
                            did(nc.vector.tensor_scalar(score[0:rows, at:at + L], e, BIG, -BIG, ALU.mult, ALU.add))
            settled()



ORDER = [t for i in range(NT // 2) for t in (NT - 1 - i, i)]


class Item:

    def __init__(self, n, tile, head, keys, sample):
        self.n, self.tile, self.head, self.keys, self.sample = n, tile, head, keys, sample
        blocks = [(k, min(P, keys - k)) for k in range(0, keys, P)]
        self.chunks = [blocks[i:i + 4] for i in range(0, len(blocks), 4)]


def number_chunks(items):
    at = 0
    for it in items:
        it.first = at
        at += len(it.chunks)
    return at


def attention(nc, ctx, pl, c, tag, items, loads, stores, pe_first, act_first, dve_first, logits, bias,
              values, out_at, pool_part=None):
    def sem(name):
        return ctx.enter_context(nc.semaphore(name))

    ident = c["ident"]
    biased = [pl(f"{tag}_biased{s}", [P, KEYS_S], F32) for s in range(2)]
    prob = [pl(f"{tag}_prob{s}", [P, KEYS_S], F32) for s in range(2)]
    probT = [pl(f"{tag}_probT{s}", [P, 4, P], F32) for s in range(2)]
    rmax = pl(f"{tag}_rmax", [P, 4], F32)
    nmax = pl(f"{tag}_nmax", [P, 4], F32)
    rsum = pl(f"{tag}_rsum", [P, 4], F32)
    rinv = pl(f"{tag}_rinv", [P, 4], F32)
    ps = ctx.enter_context(nc.psum_tensor(f"{tag}_logits", [P, 4 * 512], F32))
    pt = ctx.enter_context(nc.psum_tensor(f"{tag}_transposed", [P, 2, 512], F32))
    po = ctx.enter_context(nc.psum_tensor(f"{tag}_outputs", [P, 2, 512], F32))
    s = {k: sem(f"{tag}_{k}") for k in ("qk_done", "max_done", "biased_done", "exp_done", "item_transposed", "tr_done",
                             "probT_done", "pv_done", "item_out", "out_done", "scaled", "dve_step")}
    c["sems"] = s
    N = len(items)
    M = number_chunks(items)
    c["M"], c["N"], c["pt"], c["po"], c["ps"] = M, N, pt, po, ps
    block = ctx.enter_context(nc.Block())

    @block.sync
    def _(sp):
        loads(sp)
        stores(sp)

    @block.tensor
    def _(pe):
        pe_first(pe)

        def qk(n):
            it = items[n]
            if it.sample and n >= 1:
                pe.wait_ge(s["biased_done"], n)
            elif n >= 2:
                pe.wait_ge(s["biased_done"], n - 1)
            at = 0 if it.sample else 1024 * (n % 2)
            logits(pe, it, ps[:, at:at + it.keys]).then_inc(s["qk_done"], 1)

        def transposes(it, ci, m):
            if ci == 0:
                pe.wait_ge(s["scaled"] if it.sample else s["exp_done"], it.rank + 1 if it.sample else it.n + 1)
            if m >= 2:
                pe.wait_ge(s["probT_done"], m - 1)
            for b, (k0, kn) in enumerate(it.chunks[ci]):
                mm = nc.tensor.transpose(pt[0:kn, m % 2, b * P:(b + 1) * P], prob[it.n % 2][:, k0:k0 + kn],
                                         ident[:, :])
            mm.then_inc(s["tr_done"], 1)

        def weighted(it, ci, m):
            pe.wait_ge(s["probT_done"], m + 1)
            if ci == 0 and it.n >= 2:
                pe.wait_ge(s["out_done"], it.n - 1)
            last = ci == len(it.chunks) - 1
            heads = range(4) if it.sample else [0]
            for b, (k0, kn) in enumerate(it.chunks[ci]):
                for j in heads:
                    if it.sample:
                        out, l = po[0:NEW, it.n % 2, j * HD:(j + 1) * HD], probT[m % 2][0:kn, b, j * NEW:(j + 1) * NEW]
                    else:
                        out, l = po[:, it.n % 2, 0:HD], probT[m % 2][0:kn, b, :]
                    mm = nc.tensor.matmul(out, l, values(pe, it, j, k0, kn), start=(ci == 0 and b == 0 and j == 0),
                                          stop=(last and b == len(it.chunks[ci]) - 1),
                                          skip_group_check=it.sample)
            mm.then_inc(s["pv_done"], 1)

        for n in range(min(2, N)):
            qk(n)
        behind = None
        for it in items:
            for ci in range(len(it.chunks)):
                if ci == 0 and it.n + 2 < N:
                    qk(it.n + 2)
                transposes(it, ci, it.first + ci)
                if behind:
                    weighted(*behind)
                behind = (it, ci, it.first + ci)
        weighted(*behind)

    @block.scalar
    def _(act):
        act_first(act)

        def exp(n):
            it = items[n]
            act.wait_ge(s["max_done"], n + 1)
            if n >= 2:
                act.wait_ge(s["tr_done"], items[n - 1].first)
            if n >= 4:
                act.wait_ge(s["out_done"], n - 3)
            nc.scalar.activation(prob[n % 2][:, 0:it.keys], biased[n % 2][:, 0:it.keys], ACT.Exp,
                                 bias=nmax[:, n % 4:n % 4 + 1], accum_out=rsum[:, n % 4:n % 4 + 1])\
                .then_inc(s["exp_done"], 1)

        exp(0)
        for it in items:
            if it.n + 1 < N:
                exp(it.n + 1)
            for ci, ch in enumerate(it.chunks):
                m = it.first + ci
                act.wait_ge(s["tr_done"], m + 1)
                if m >= 2:
                    act.wait_ge(s["pv_done"], m - 1)
                full = sum(kn == P for _, kn in ch)
                if full:
                    last = nc.scalar.copy(probT[m % 2][:, 0:full, :],
                                          pt[:, m % 2, 0:full * P].rearrange("p (b r) -> p b r", r=P))
                if full < len(ch):
                    kn = ch[full][1]
                    last = nc.scalar.copy(probT[m % 2][0:kn, full, :], pt[0:kn, m % 2, full * P:(full + 1) * P])
                last.then_inc(s["probT_done"], 1)

    @block.vector
    def _(dve):
        steps = [0]
        dve_first(dve)

        def biased_max(n):
            it = items[n]
            at = 0 if it.sample else 1024 * (n % 2)
            in1 = bias(dve, it)
            dve.wait_ge(s["qk_done"], n + 1)
            if n >= 2:
                dve.wait_ge(s["exp_done"], n - 1)
            nc.vector.tensor_tensor_reduce(biased[n % 2][:, 0:it.keys], ps[:, at:at + it.keys], in1, 1.0, -3.3e38,
                                           ALU.add, ALU.max, rmax[:, n % 4:n % 4 + 1]).then_inc(s["biased_done"], 1)
            dve.wait_ge(s["biased_done"], n + 1)
            nc.vector.tensor_scalar(nmax[:, n % 4:n % 4 + 1], rmax[:, n % 4:n % 4 + 1], -1.0, None, ALU.mult)\
                .then_inc(s["max_done"], 1)

        def finish(n):
            it = items[n]
            if it.sample:
                dve.wait_ge(s["pv_done"], it.first + len(it.chunks))
                for j in range(4):
                    last = nc.vector.tensor_copy(out_at(it, j), po[0:NEW, n % 2, j * HD:(j + 1) * HD])
                last.then_inc(s["out_done"], 1)
                return
            dve.wait_ge(s["exp_done"], n + 1)
            nc.vector.reciprocal(rinv[:, n % 4:n % 4 + 1], rsum[:, n % 4:n % 4 + 1]).then_inc(s["dve_step"], 1)
            steps[0] += 1
            dve.wait_ge(s["dve_step"], steps[0])
            dve.wait_ge(s["pv_done"], it.first + len(it.chunks))
            nc.vector.tensor_scalar(out_at(it, 0), po[:, n % 2, 0:HD], rinv[:, n % 4:n % 4 + 1], None, ALU.mult)\
                .then_inc(s["out_done"], 1)

        def scale_sample(n):
            it = items[n]
            dve.wait_ge(s["exp_done"], n + 1)
            nc.vector.reciprocal(rinv[:, n % 4:n % 4 + 1], rsum[:, n % 4:n % 4 + 1]).then_inc(s["dve_step"], 1)
            steps[0] += 1
            dve.wait_ge(s["dve_step"], steps[0])
            nc.vector.tensor_scalar(prob[n % 2][:, 0:it.keys], prob[n % 2][:, 0:it.keys], rinv[:, n % 4:n % 4 + 1],
                                    None, ALU.mult).then_inc(s["scaled"], 1)

        for n in range(min(2, N)):
            biased_max(n)
        for n in range(N):
            if items[n].sample:
                scale_sample(n)
            if n + 2 < N:
                biased_max(n + 2)
            if n >= 1:
                finish(n - 1)
        finish(N - 1)

    if pool_part:
        @block.gpsimd
        def _(pool):
            pool_part(pool)



def fox(nc, d, c):
    from contextlib import ExitStack
    with ExitStack() as ctx:
        def sem(name):
            return ctx.enter_context(nc.semaphore(name))

        pl = Places(nc, c["after_mix"], c["end"])
        v = pl("fox_v", [P, NT, 512], F32)
        v_past = pl("fox_v_past", [P, NT, 512], F32)
        v_new = pl("fox_v_new", [NEW, 512], F32)
        kT_past = pl("fox_kT_past", [P, 2, PAST], F32)
        kT_new = pl("fox_kT_new", [P, 4, NEW], F32)
        q_diag = pl("q_diag", [P, 4, P], F32)
        key_bias = [pl(f"key_bias{s}", [P, SEQ], F32) for s in range(2)]
        key_bias_s = pl("key_bias_s", [P, KEYS_S], F32)
        kT_hi, kT_lo, qT_hi, qT_lo = c["kT_hi"], c["kT_lo"], c["qT_hi"], c["qT_lo"]
        mix, logf, ident = c["mix"], c["logf"], c["ident"]
        m0 = Places(nc, c["rest"], c["after_mix"])
        ones = m0("ones", [FOX_H, SEQ], F32)
        negc = m0("negc", [FOX_H, SEQ], F32)
        bias_s = m0("bias_s", [FOX_H, KEYS_S], F32)
        lf_past = m0("lf_past", [FOX_H, PAST], F32)

        items = [Item(8 * h + i, t, h, (t + 1) * P, False) for h in range(FOX_H) for i, t in enumerate(ORDER)]
        items += [Item(64 + q, NT, 4 * q, KEYS_S, True) for q in range(2)]
        for it in items:
            it.rank = it.n - 64
        lf_loaded, v_loaded, vs_loaded = sem("lf_loaded"), sem("v_loaded"), sem("vs_loaded")
        kp_loaded, bias_stored = sem("kp_loaded"), sem("bias_stored")
        kb_loaded = [sem(f"kb_loaded{s}") for s in range(2)]
        kbs_loaded, kbs_ready = sem("kbs_loaded"), sem("kbs_ready")
        lfT_done, c_done, start_step, diag_done = sem("lfT_done"), sem("c_done"), sem("start_step"), sem("diag_done")
        S = c

        def loads(sp):
            s = S["sems"]
            sp.dma_start(lf_past[:, :], d["past_logfT"]).then_inc(lf_loaded, 16)
            sp.dma_start(v[:, :, :], d["fv"][0:SEQ, :].rearrange("(t p) n -> p t n", p=P)).then_inc(v_loaded, 16)
            sp.wait_ge(c_done, 3)
            sp.dma_start(d["negc"], negc[:, :]).then_inc(bias_stored, 16)
            sp.dma_start(d["bias_s"], bias_s[:, :]).then_inc(bias_stored, 16)
            sp.wait_ge(bias_stored, 32)
            for h in range(FOX_H):
                if h >= 2:
                    sp.wait_ge(s["biased_done"], 8 * (h - 1))
                sp.dma_start(key_bias[h % 2][:, :], d["negc"][h].partition_broadcast(P)).then_inc(kb_loaded[h % 2], 16)
                if h == 1:
                    sp.dma_start(v_past[:, :, :], d["past_fv"].rearrange("(t p) n -> p t n", p=P)).then_inc(vs_loaded, 16)
                    sp.dma_start(v_new[:, :], d["fv"][SEQ:ROWS, :]).then_inc(vs_loaded, 16)
            for q in range(2):
                if q:
                    sp.wait_ge(s["biased_done"], 65)
                sp.dma_start(kT_past[:, :, :], d["past_fkT"][q * 256:(q + 1) * 256, :].rearrange(
                    "(a p) n -> p a n", p=P)).then_inc(kp_loaded, 16)
                for j in range(4):
                    sp.dma_start(key_bias_s[j * NEW:(j + 1) * NEW, :], d["bias_s"][4 * q + j].partition_broadcast(NEW))\
                        .then_inc(kbs_loaded, 16)

        def stores(sp):
            sp.wait_ge(S["sems"]["out_done"], len(items))

        def pe_first(pe):
            ps = S["ps"]
            for t, r0, rows in TILES:
                at = r0 if t < NT else SEQ
                mm = nc.tensor.transpose(ps[0:FOX_H, at:at + rows], logf[0:rows, t, :], ident[0:rows, 0:rows])
            mm.then_inc(lfT_done, 1)
            pe.wait_ge(c_done, 4)
            pe.wait_ge(diag_done, 1)

        def dve_first(dve):
            ps = S["ps"]
            nc.vector.memset(ones[:, :], 1.0).then_inc(start_step, 1)
            nc.vector.memset(q_diag[:, :, :], 0.0).then_inc(start_step, 1)
            nc.vector.memset(bias_s[:, PAST - 1:PAST], 0.0).then_inc(start_step, 1)
            dve.wait_ge(start_step, 3)
            dve.wait_ge(lf_loaded, 16)
            nc.vector.tensor_tensor_scan(bias_s[:, 0:PAST - 1][:, ::-1], ones[:, 0:PAST - 1], lf_past[:, 1:PAST][:, ::-1],
                                         0.0, ALU.mult, ALU.add).then_inc(c_done, 1)
            dve.wait_ge(lfT_done, 1)
            nc.vector.tensor_tensor_scan(negc[:, :], ones[:, :], ps[0:FOX_H, 0:SEQ], 0.0, ALU.mult, ALU.subtract)\
                .then_inc(c_done, 1)
            nc.vector.tensor_tensor_scan(bias_s[:, PAST:KEYS_S], ones[:, 0:NEW], ps[0:FOX_H, SEQ:ROWS], 0.0, ALU.mult,
                                         ALU.subtract).then_inc(c_done, 1)
            nc.vector.tensor_tensor(kT_new[:, :, :], f32(kT_hi[:, :, SEQ:ROWS]), f32(kT_lo[:, :, SEQ:ROWS]), ALU.add)\
                .then_inc(c_done, 1)
            for a in range(4):
                for r in range(2):
                    part = slice(r * HD, (r + 1) * HD)
                    col = ((2 * a + r) % 4) * NEW
                    last = nc.vector.tensor_tensor(q_diag[part, a, col:col + NEW], f32(qT_hi[part, a, SEQ:ROWS]),
                                                   f32(qT_lo[part, a, SEQ:ROWS]), ALU.add)
            last.then_inc(diag_done, 1)

        def bias(dve, it):
            if not it.sample:
                dve.wait_ge(kb_loaded[it.head % 2], 16 * (it.head // 2 + 1))
                return key_bias[it.head % 2][:, 0:it.keys]
            q = it.head // 4
            dve.wait_ge(kbs_loaded, 64 * (q + 1))
            return key_bias_s[:, :]

        def logits(pe, it, out):
            if not it.sample:
                part, a = slice(HD * (it.head % 2), HD * (it.head % 2) + HD), it.head // 2
                qs = slice(it.tile * P, (it.tile + 1) * P)
                for k0 in range(0, it.keys, 512):
                    ks = slice(k0, min(it.keys, k0 + 512))
                    o = out[:, ks]
                    nc.tensor.matmul(o, qT_hi[part, a, qs], kT_hi[part, a, ks], start=True, stop=False)
                    nc.tensor.matmul(o, qT_hi[part, a, qs], kT_lo[part, a, ks], start=False, stop=False)
                    mm = nc.tensor.matmul(o, qT_lo[part, a, qs], kT_hi[part, a, ks], start=False, stop=ks.stop < it.keys)
                return nc.tensor.matmul(out[:, it.keys - P:it.keys], c["ident16"][:, :], c["causal16"][:, :],
                                        start=False, stop=True)
            q = it.head // 4
            pe.wait_ge(kp_loaded, 16 * (q + 1))
            for k0 in range(0, PAST, 512):
                for a in range(2):
                    nc.tensor.matmul(out[:, k0:k0 + 512], q_diag[:, 2 * q + a, :], kT_past[:, a, k0:k0 + 512],
                                     start=a == 0, stop=a == 1)
            for a in range(2):
                nc.tensor.matmul(out[:, PAST:KEYS_S], q_diag[:, 2 * q + a, :], kT_new[:, 2 * q + a, :],
                                 start=a == 0, stop=False)
            return nc.tensor.matmul(out[:, PAST:KEYS_S], c["ident16"][:, :], c["causal_s16"][:, :], start=False, stop=True)

        def values(pe, it, j, k0, kn):
            h = it.head + j
            cols = slice(h * HD, (h + 1) * HD)
            if not it.sample:
                if it.n == 0 and k0 == 0:
                    pe.wait_ge(v_loaded, 16)
                return v[:, k0 // P, cols]
            if it.n == 64 and k0 == 0 and j == 0:
                pe.wait_ge(vs_loaded, 32)
            return v_past[:, k0 // P, cols] if k0 < PAST else v_new[0:kn, cols]

        def out_at(it, j):
            h = it.head + j
            rows = NEW if it.sample else P
            return mix[0:rows, it.tile, h * HD:(h + 1) * HD]

        attention(nc, ctx, pl, c, "fox", items, loads, stores, pe_first, lambda act: None, dve_first, logits, bias,
                  values, out_at)



def dsa(nc, d, c):
    from contextlib import ExitStack
    with ExitStack() as ctx:
        def sem(name):
            return ctx.enter_context(nc.semaphore(name))

        pl = Places(nc, c["after_mix"], c["end"])
        q_row = pl("dsa_q_row", [P, NT + 1, 512], F32)
        k_row = pl("dsa_k_row", [P, NT + 1, 2 * P], F32)
        v = pl("dsa_v", [P, NT, P], F32)
        v_past = pl("dsa_v_past", [P, NT, P], F32)
        v_new = pl("dsa_v_new", [NEW, P], F32)
        kT_past = pl("dsa_kT_past", [P, 2, PAST], F32)
        kT_new = pl("dsa_kT_new", [P, 2, NEW], F32)
        q_diag = pl("dsa_q_diag", [P, 4, P], F32)
        mask_s = pl("mask_s", [P, KEYS_S], F32)
        kT_hi, kT_lo, qT_hi, qT_lo = c["kT_hi"], c["kT_lo"], c["qT_hi"], c["qT_lo"]
        mix, ident, score, corner = c["mix"], c["ident"], c["score"], c["corner"]

        items = [Item(8 * h + i, t, h, (t + 1) * P, False) for h in range(DSA_H) for i, t in enumerate(ORDER)]
        items += [Item(64 + q, NT, 4 * q, KEYS_S, True) for q in range(2)]
        for it in items:
            it.rank = it.n - 64
        q_loaded, k_loaded, v_loaded, vs_loaded = sem("q_loaded"), sem("k_loaded"), sem("v_loaded"), sem("vs_loaded")
        kp_loaded, mask_loaded = sem("kp_loaded"), sem("mask_loaded")
        h_tr, h_hi, h_lo, diag_done, zeroed = sem("h_tr"), sem("h_hi"), sem("h_lo"), sem("diag_done"), sem("zeroed")
        S = c

        def loads(sp):
            for r in range(2):
                for g in range(KV_H):
                    at = (2 * g + r) * HD
                    sp.dma_start(k_row[:, 0:NT, at:at + HD], d["dk"][0:SEQ, g * HD:(g + 1) * HD].rearrange(
                        "(t p) n -> p t n", p=P)).then_inc(k_loaded, 16)
                    sp.dma_start(k_row[0:NEW, NT, at:at + HD], d["dk"][SEQ:ROWS, g * HD:(g + 1) * HD])\
                        .then_inc(k_loaded, 16)
            sp.dma_start(q_row[:, 0:NT, :], d["dq"][0:SEQ, :].rearrange("(t p) n -> p t n", p=P)).then_inc(q_loaded, 16)
            sp.dma_start(q_row[0:NEW, NT, :], d["dq"][SEQ:ROWS, :]).then_inc(q_loaded, 16)
            sp.dma_start(v[:, :, :], d["dv"][0:SEQ, :].rearrange("(t p) n -> p t n", p=P)).then_inc(v_loaded, 16)
            sp.dma_start(v_past[:, :, :], d["past_dv"].rearrange("(t p) n -> p t n", p=P)).then_inc(vs_loaded, 16)
            sp.dma_start(v_new[:, :], d["dv"][SEQ:ROWS, :]).then_inc(vs_loaded, 16)
            for r in range(2):
                for g in range(KV_H):
                    sp.dma_start(kT_past[r * HD:(r + 1) * HD, g, :], d["past_dkT"][g * HD:(g + 1) * HD, :])\
                        .then_inc(kp_loaded, 16)
            at = SEG[-1][1]
            for j in range(4):
                sp.dma_start(mask_s[j * NEW:(j + 1) * NEW, :], score[0:NEW, at:at + KEYS_S]).then_inc(mask_loaded, 16)

        def stores(sp):
            sp.wait_ge(S["sems"]["out_done"], len(items))

        def pe_first(pe):
            ps = S["ps"]
            pe.wait_ge(k_loaded, 16 * 8)
            pe.wait_ge(q_loaded, 32)
            for t, r0, rows in TILES:
                if t >= 2:
                    pe.wait_ge(h_lo, t - 1)
                o = 1024 * (t % 2)
                for a in range(4):
                    nc.tensor.transpose(ps[:, o + a * P:o + a * P + rows], q_row[0:rows, t, a * P:(a + 1) * P],
                                        ident[0:rows, 0:rows])
                for g in range(2):
                    mm = nc.tensor.transpose(ps[:, o + 512 + g * P:o + 512 + g * P + rows],
                                             k_row[0:rows, t, g * P:(g + 1) * P], ident[0:rows, 0:rows])
                mm.then_inc(h_tr, 1)
            pe.wait_ge(h_lo, NT + 1)
            pe.wait_ge(diag_done, 2)

        def views(t, r0, rows):
            o = 1024 * (t % 2)
            q = S["ps"][:, o:o + 512].rearrange("p (a r) -> p a r", r=P)[:, :, 0:rows]
            k = S["ps"][:, o + 512:o + 768].rearrange("p (a r) -> p a r", r=P)[:, :, 0:rows]
            return q, k, slice(r0, r0 + rows)

        def act_first(act):
            for t, r0, rows in TILES:
                q, k, cols = views(t, r0, rows)
                act.wait_ge(h_tr, t + 1)
                nc.scalar.activation(qT_hi[:, :, cols], q, ACT.Copy, scale=SCALE)
                nc.scalar.copy(kT_hi[:, 0:2, cols], k).then_inc(h_hi, 1)

        def dve_first(dve):
            nc.vector.memset(q_diag[:, :, :], 0.0).then_inc(zeroed, 1)
            for t, r0, rows in TILES:
                q, k, cols = views(t, r0, rows)
                dve.wait_ge(h_hi, t + 1)
                nc.vector.scalar_tensor_tensor(qT_lo[:, :, cols], q, SCALE, f32(qT_hi[:, :, cols]), ALU.mult,
                                               ALU.subtract)
                nc.vector.tensor_tensor(kT_lo[:, 0:2, cols], k, f32(kT_hi[:, 0:2, cols]), ALU.subtract)\
                    .then_inc(h_lo, 1)
            dve.wait_ge(h_lo, NT + 1)
            dve.wait_ge(zeroed, 1)
            nc.vector.tensor_tensor(kT_new[:, :, :], f32(kT_hi[:, 0:2, SEQ:ROWS]), f32(kT_lo[:, 0:2, SEQ:ROWS]), ALU.add)\
                .then_inc(diag_done, 1)
            for a in range(4):
                for r in range(2):
                    part = slice(r * HD, (r + 1) * HD)
                    col = ((2 * a + r) % 4) * NEW
                    last = nc.vector.tensor_tensor(q_diag[part, a, col:col + NEW], f32(qT_hi[part, a, SEQ:ROWS]),
                                                   f32(qT_lo[part, a, SEQ:ROWS]), ALU.add)
            last.then_inc(diag_done, 1)

        def bias(dve, it):
            if it.sample:
                dve.wait_ge(mask_loaded, 64)
                return mask_s[:, :]
            if it.keys <= TOPK:
                return corner[:, 2 * P - it.keys:2 * P]
            at = SEG[it.tile - TOPK // P][1]
            return score[:, at:at + it.keys]

        def logits(pe, it, out):
            g = it.head // 4
            if not it.sample:
                part, a = slice(HD * (it.head % 2), HD * (it.head % 2) + HD), it.head // 2
                qs = slice(it.tile * P, (it.tile + 1) * P)
                for k0 in range(0, it.keys, 512):
                    ks = slice(k0, min(it.keys, k0 + 512))
                    o = out[:, ks]
                    nc.tensor.matmul(o, qT_hi[part, a, qs], kT_hi[part, g, ks], start=True, stop=False)
                    nc.tensor.matmul(o, qT_hi[part, a, qs], kT_lo[part, g, ks], start=False, stop=False)
                    mm = nc.tensor.matmul(o, qT_lo[part, a, qs], kT_hi[part, g, ks], start=False, stop=True)
                return mm
            if it.n == 64:
                pe.wait_ge(kp_loaded, 64)
            for k0 in list(range(0, PAST, 512)) + [PAST]:
                k1 = min(k0 + 512, KEYS_S)
                for a in range(2):
                    r = kT_past[:, g, k0:k1] if k0 < PAST else kT_new[:, g, :]
                    mm = nc.tensor.matmul(out[:, k0:k1], q_diag[:, 2 * g + a, :], r, start=a == 0, stop=a == 1)
            return mm

        def values(pe, it, j, k0, kn):
            h = it.head + j
            cols = slice(h // 4 * HD, h // 4 * HD + HD)
            if not it.sample:
                if it.n == 0 and k0 == 0:
                    pe.wait_ge(v_loaded, 16)
                return v[:, k0 // P, cols]
            if it.n == 64 and k0 == 0 and j == 0:
                pe.wait_ge(vs_loaded, 32)
            return v_past[:, k0 // P, cols] if k0 < PAST else v_new[0:kn, cols]

        def out_at(it, j):
            h = it.head + j
            rows = NEW if it.sample else P
            return mix[0:rows, it.tile, 512 + h * HD:512 + (h + 1) * HD]

        attention(nc, ctx, pl, c, "dsa", items, loads, stores, pe_first, act_first, dve_first, logits, bias,
                  values, out_at)



class Norm:

    def __init__(self, nc, pl, sem, tag, gain, shift, loaded):
        self.nc, self.gain, self.shift, self.loaded = nc, gain, shift, loaded
        self.stats = pl(tag + "_stats", [P, NT + 1, 12], F32)
        self.mv = pl(tag + "_mv", [P, NT + 1, 2], F32)
        self.ve = pl(tag + "_var_eps", [P, NT + 1], F32)
        self.rstd = pl(tag + "_rstd", [P, NT + 1], F32)
        self.power = pl(tag + "_power", [P, 1], F32)
        self.step, self.var_done, self.rstd_done = sem("ln_step"), sem("ln_var_done"), sem("ln_rstd_done")
        self.n = 0

    def settled(self, dve, ins):
        self.n += 1
        ins.then_inc(self.step, 1)
        dve.wait_ge(self.step, self.n)

    def moments(self, dve, t, rows, y):
        v = self.nc.vector
        v.bn_stats(self.stats[0:rows, t, 0:6], y[:, 0:512])
        self.settled(dve, v.bn_stats(self.stats[0:rows, t, 6:12], y[:, 512:D]))
        self.settled(dve, v.bn_aggr(self.mv[0:rows, t, :], self.stats[0:rows, t, :]))
        v.tensor_scalar(self.ve[0:rows, t:t + 1], self.mv[0:rows, t, 1:2], LN_EPS, None, ALU.add)\
            .then_inc(self.var_done, 1)

    def power_first(self):
        self.nc.gpsimd.memset(self.power[:, :], -0.5).then_inc(self.rstd_done, 1)

    def root(self, pool, t, rows):
        pool.wait_ge(self.rstd_done, 1)
        pool.wait_ge(self.var_done, t + 1)
        self.nc.gpsimd.tensor_tensor(self.rstd[0:rows, t:t + 1], self.ve[0:rows, t:t + 1], self.power[0:rows, :],
                                     ALU.pow).then_inc(self.rstd_done, 1)

    def scaled(self, dve, t, rows, y):
        dve.wait_ge(self.rstd_done, t + 2)
        dve.wait_ge(self.loaded, 32)
        v = self.nc.vector
        self.settled(dve, v.tensor_scalar(y, y, self.mv[0:rows, t, 0:1], self.rstd[0:rows, t:t + 1], ALU.subtract,
                                          ALU.mult))
        return v.tensor_tensor(y, y, self.gain[0:rows, :], ALU.mult)



def mix_out(nc, d, c):
    from contextlib import ExitStack
    with ExitStack() as ctx:
        def sem(name):
            return ctx.enter_context(nc.semaphore(name))

        tp = Places(nc, c["t_region"], c["rest"])
        w_hi = tp("wo_hi", [P, KD, D], F32R)
        w_lo = tp("wo_lo", [P, KD, D], F32R)
        pl = Places(nc, c["after_mix"], c["end"])
        w_raw = [pl(f"wo_raw{s}", [P, D], F32) for s in range(4)]
        mT_hi = [pl(f"mT_hi{s}", [P, KD, P], F32R) for s in range(2)]
        mT_lo = [pl(f"mT_lo{s}", [P, KD, P], F32R) for s in range(2)]
        x_row = [pl(f"x_row{s}", [P, D], F32) for s in range(2)]
        pre = [pl(f"pre{s}", [P, D], F32) for s in range(2)]
        gain, shift = pl("ln1_gain", [P, D], F32), pl("ln1_shift", [P, D], F32)
        mix, ident = c["mix"], c["ident"]
        pt = ctx.enter_context(nc.psum_tensor("mix_T", [P, 4 * 512], F32))
        py = ctx.enter_context(nc.psum_tensor("mixed", [P, 4 * 512], F32))
        w_loaded = [sem(f"wo_loaded{s}") for s in range(4)]
        x_loaded = [sem(f"x_row_loaded{s}") for s in range(2)]
        w_hi_done, w_lo_done, ln_loaded = sem("w_hi_done"), sem("w_lo_done"), sem("ln_loaded")
        tr_done, m_hi, m_lo = sem("mix_transposed"), sem("m_hi"), sem("m_lo")
        product, pre_done, h_done = sem("product"), sem("pre_done"), sem("h_done")
        norm = Norm(nc, pl, sem, "ln1", gain, shift, ln_loaded)
        block = ctx.enter_context(nc.Block())

        @block.sync
        def _(sp):
            def load_x(t):
                _, r0, rows = TILES[t]
                if t >= 2:
                    sp.wait_ge(pre_done, t - 1)
                sp.dma_start(x_row[t % 2][0:rows, :], d["x"][r0:r0 + rows, :]).then_inc(x_loaded[t % 2], 16)

            for k in range(KD):
                if k >= 4:
                    sp.wait_ge(w_lo_done, k - 3)
                sp.dma_start(w_raw[k % 4][:, :], d["w_out"][k * P:(k + 1) * P, :]).then_inc(w_loaded[k % 4], 16)
            load_x(0)
            load_x(1)
            sp.dma_start(gain[:, :], d["ln1_g"].partition_broadcast(P)).then_inc(ln_loaded, 16)
            sp.dma_start(shift[:, :], d["ln1_b"].partition_broadcast(P)).then_inc(ln_loaded, 16)
            for t in range(2, NT + 1):
                load_x(t)
            sp.wait_ge(h_done, NT + 1)

        @block.tensor
        def _(pe):
            def transposes(t):
                _, r0, rows = TILES[t]
                if t >= 2:
                    pe.wait_ge(m_lo, t - 1)
                for k in range(KD):
                    o = 1024 * (t % 2) + k * P
                    mm = nc.tensor.transpose(pt[:, o:o + rows], mix[0:rows, t, k * P:(k + 1) * P],
                                             ident[0:rows, 0:rows])
                mm.then_inc(tr_done, 1)

            transposes(0)
            for t, r0, rows in TILES:
                if t < NT:
                    transposes(t + 1)
                pe.wait_ge(m_lo, t + 1)
                if t >= 2:
                    pe.wait_ge(pre_done, t - 1)
                for half in range(2):
                    cols = slice(512 * half, 512 * half + 512)
                    out = py[0:rows, 1024 * (t % 2) + 512 * half:1024 * (t % 2) + 512 * half + 512]
                    for k in range(KD):
                        if t == 0 and half == 0:
                            pe.wait_ge(w_lo_done, k + 1)
                        mh, ml = mT_hi[t % 2][:, k, 0:rows], mT_lo[t % 2][:, k, 0:rows]
                        for i, (l, r) in enumerate([(mh, w_hi[:, k, cols]), (mh, w_lo[:, k, cols]),
                                                    (ml, w_hi[:, k, cols])]):
                            mm = nc.tensor.matmul(out, l, r, start=(k == 0 and i == 0), stop=(k == KD - 1 and i == 2))
                mm.then_inc(product, 1)

        @block.scalar
        def _(act):
            def mix_hi(t):
                _, r0, rows = TILES[t]
                act.wait_ge(tr_done, t + 1)
                if t >= 2:
                    act.wait_ge(product, t - 1)
                o = 1024 * (t % 2)
                nc.scalar.copy(mT_hi[t % 2][:, :, 0:rows],
                               pt[:, o:o + 1024].rearrange("p (k r) -> p k r", r=P)[:, :, 0:rows]).then_inc(m_hi, 1)

            for k in range(KD):
                if k == 1:
                    mix_hi(0)
                act.wait_ge(w_loaded[k % 4], 16 * (k // 4 + 1))
                nc.scalar.copy(w_hi[:, k, :], w_raw[k % 4][:, :]).then_inc(w_hi_done, 1)
            for t in range(1, NT + 1):
                mix_hi(t)

        @block.gpsimd
        def _(pool):
            norm.power_first()
            for t, r0, rows in TILES:
                norm.root(pool, t, rows)

        @block.vector
        def _(dve):
            def mix_lo(t):
                _, r0, rows = TILES[t]
                dve.wait_ge(m_hi, t + 1)
                o = 1024 * (t % 2)
                nc.vector.tensor_tensor(mT_lo[t % 2][:, :, 0:rows],
                                        pt[:, o:o + 1024].rearrange("p (k r) -> p k r", r=P)[:, :, 0:rows],
                                        f32(mT_hi[t % 2][:, :, 0:rows]), ALU.subtract).then_inc(m_lo, 1)

            def finish(t):
                _, r0, rows = TILES[t]
                y = pre[t % 2][0:rows, :]
                norm.settled(dve, norm.scaled(dve, t, rows, y))
                nc.vector.tensor_tensor(mix[0:rows, t, :], y, shift[0:rows, :], ALU.add).then_inc(h_done, 1)

            for k in range(KD):
                if k == 1:
                    mix_lo(0)
                dve.wait_ge(w_hi_done, k + 1)
                nc.vector.tensor_tensor(w_lo[:, k, :], w_raw[k % 4][:, :], f32(w_hi[:, k, :]), ALU.subtract)\
                    .then_inc(w_lo_done, 1)
            mix_lo(1)
            for t, r0, rows in TILES:
                dve.wait_ge(x_loaded[t % 2], 16 * (t // 2 + 1))
                dve.wait_ge(product, t + 1)
                if t >= 2:
                    dve.wait_ge(h_done, t - 1)
                y = pre[t % 2][0:rows, :]
                nc.vector.scalar_tensor_tensor(y, x_row[t % 2][0:rows, :], ALPHA,
                                               py[0:rows, 1024 * (t % 2):1024 * (t % 2) + D], ALU.mult, ALU.add)\
                    .then_inc(pre_done, 1)
                if t + 2 <= NT:
                    mix_lo(t + 2)
                dve.wait_ge(pre_done, t + 1)
                norm.moments(dve, t, rows, y)
                if t >= 1:
                    finish(t - 1)
            finish(NT)



def ffn(nc, d, c):
    from contextlib import ExitStack
    with ExitStack() as ctx:
        def sem(name):
            return ctx.enter_context(nc.semaphore(name))

        NB = D_FF // (2 * P)
        NU = 2 * (NT + 1)
        tp = Places(nc, c["t_region"], c["rest"])
        h_hi = tp("h_hi", [P, KD, ROWS], F32R)
        h_lo = tp("h_lo", [P, KD, ROWS], F32R)
        sp_ = Places(nc, -(-nc.sbuf_base // 64) * 64, c["t_region"])
        g_raw = sp_("gate_raw", [P, KD, 2 * P], F32)
        u_raw = sp_("up_raw", [P, KD, 2 * P], F32)
        pl = Places(nc, c["after_mix"], c["end"])
        d_raw = pl("down_raw", [P, 2, D], F32)
        w_hi = [pl(f"gu_hi{s}", [P, KD, P], F32R) for s in range(2)]
        w_lo = [pl(f"gu_lo{s}", [P, KD, P], F32R) for s in range(2)]
        d_hi = pl("down_hi", [P, 2, D], F32R)
        d_lo = pl("down_lo", [P, 2, D], F32R)
        a_hi = pl("act_hi", [P, 2, ROWS], F32R)
        a_lo = pl("act_lo", [P, 2, ROWS], F32R)
        gated = pl("gated", [P, ROWS], F32)
        prod = pl("prod", [P, ROWS], F32)
        gain, shift = pl("ln2_gain", [P, D], F32), pl("ln2_shift", [P, D], F32)
        y, ident = c["mix"], c["ident"]
        pg = ctx.enter_context(nc.psum_tensor("gate", [P, 3, 512], F32))
        pu = ctx.enter_context(nc.psum_tensor("up", [P, 3, 512], F32))
        pd = ctx.enter_context(nc.psum_tensor("down", [P, 2, 512], F32))
        hT_banks = [pg[:, 0, :], pg[:, 1, :], pu[:, 0, :], pu[:, 1, :]]

        g_loaded, u_loaded, d_loaded, ln_loaded = sem("g_loaded"), sem("u_loaded"), sem("d_loaded"), sem("ln_loaded")
        h_tr, h_hi_done, h_lo_done, y_ready = sem("h_tr"), sem("h_hi_done"), sem("h_lo_done"), sem("y_ready")
        w_hi_done, w_lo_done, d_hi_done, d_lo_done = (sem("w_hi_done"), sem("w_lo_done"), sem("d_hi_done"),
                                                      sem("d_lo_done"))
        tile_done, silu_done, prod_done = sem("tile_done"), sem("silu_done"), sem("prod_done")
        a_hi_done, a_lo_done, piece_done, added, down_done = (sem("a_hi_done"), sem("a_lo_done"), sem("piece_done"),
                                                              sem("added"), sem("down_done"))
        scaled_done, shifted, y_stored = sem("scaled_done"), sem("shifted"), sem("y_stored")
        norm = Norm(nc, pl, sem, "ln2", gain, shift, ln_loaded)
        block = ctx.enter_context(nc.Block())

        def blocks(engine, body):
            body(0, True, False)
            with engine.Fori(1, NB - 1) as b:
                body(b, False, False)
            body(NB - 1, False, True)

        @block.sync
        def _(sp):
            def body(b, first, last):
                if not first:
                    sp.wait_ge(w_lo_done, 4 * b - 1)
                sp.dma_start(g_raw[:, :, :], d["w_gate"][:, bass.ds(b * 256, 256)].rearrange(
                    "(k p) n -> p k n", p=P)).then_inc(g_loaded, 16)
                if not first:
                    sp.wait_ge(w_lo_done, 4 * b)
                sp.dma_start(u_raw[:, :, :], d["w_up"][:, bass.ds(b * 256, 256)].rearrange(
                    "(k p) n -> p k n", p=P)).then_inc(u_loaded, 16)
                if not first:
                    sp.wait_ge(d_lo_done, b)
                sp.dma_start(d_raw[:, :, :], d["w_down"][bass.ds(b * 256, 256), :].rearrange(
                    "(f p) n -> p f n", p=P)).then_inc(d_loaded, 16)

            blocks(sp, body)
            sp.dma_start(gain[:, :], d["ln2_g"].partition_broadcast(P)).then_inc(ln_loaded, 16)
            sp.dma_start(shift[:, :], d["ln2_b"].partition_broadcast(P)).then_inc(ln_loaded, 16)
            for t, r0, rows in TILES:
                sp.wait_ge(shifted, t + 1)
                sp.dma_start(d["y"][r0:r0 + rows, :], y[0:rows, t, :]).then_inc(y_stored, 16)
            sp.wait_ge(y_stored, 16 * (NT + 1))

        @block.tensor
        def _(pe):
            for q in range(2 * (NT + 1)):
                t, half = q // 2, q % 2
                rows = TILES[t][2]
                if q >= 4:
                    pe.wait_ge(h_lo_done, q - 3)
                for j in range(4):
                    k = 4 * half + j
                    mm = nc.tensor.transpose(hT_banks[q % 4][:, j * P:j * P + rows], y[0:rows, t, k * P:(k + 1) * P],
                                             ident[0:rows, 0:rows])
                mm.then_inc(h_tr, 1)
            pe.wait_ge(h_lo_done, 2 * (NT + 1))

            def tile(bank, w, slot):
                pe.wait_ge(w_lo_done, w + 1)
                for ch in range(NCH):
                    rows = slice(ch * TC, (ch + 1) * TC)
                    for k in range(KD):
                        wh, wl = w_hi[slot][:, k, :], w_lo[slot][:, k, :]
                        for i, (l, r) in enumerate([(wh, h_hi[:, k, rows]), (wh, h_lo[:, k, rows]),
                                                    (wl, h_hi[:, k, rows])]):
                            mm = nc.tensor.matmul(bank[:, ch, 0:TC], l, r, start=(k == 0 and i == 0),
                                                  stop=(k == KD - 1 and i == 2))
                mm.then_inc(tile_done, 1)

            def down(b, first):
                pe.wait_ge(a_lo_done, 2 * b + 2)
                pe.wait_ge(d_lo_done, b + 1)
                for i in range(NU):
                    t, half = i // 2, i % 2
                    _, r0, rows = TILES[t]
                    if not first or i >= 2:
                        pe.wait_ge(added, b * NU + i - 1)
                    n = 0
                    for f in range(2):
                        ah, al = a_hi[:, f, r0:r0 + rows], a_lo[:, f, r0:r0 + rows]
                        cols = slice(512 * half, 512 * half + 512)
                        for l, r in [(ah, d_hi[:, f, cols]), (ah, d_lo[:, f, cols]), (al, d_hi[:, f, cols])]:
                            mm = nc.tensor.matmul(pd[0:rows, i % 2, :], l, r, start=n == 0, stop=n == 5)
                            n += 1
                    mm.then_inc(piece_done, 1)

            tile(pg, 0, 0)

            def body(b, first, last):
                if not first:
                    pe.wait_ge(prod_done, 2 * b)
                tile(pu, 4 * b + 1, 1)
                pe.wait_ge(silu_done, 2 * b + 1)
                tile(pg, 4 * b + 2, 0)
                pe.wait_ge(prod_done, 2 * b + 1)
                tile(pu, 4 * b + 3, 1)
                if not last:
                    pe.wait_ge(silu_done, 2 * b + 2)
                    tile(pg, 4 * b + 4, 0)
                down(b, first)

            blocks(pe, body)

        def raw_of(i):
            f = i // 2 % 2
            return (g_raw if i % 2 == 0 else u_raw)[:, :, f * P:(f + 1) * P]

        @block.scalar
        def _(act):
            for q in range(2 * (NT + 1)):
                t, half = q // 2, q % 2
                _, r0, rows = TILES[t]
                act.wait_ge(h_tr, q + 1)
                nc.scalar.copy(h_hi[:, 4 * half:4 * half + 4, r0:r0 + rows],
                               hT_banks[q % 4].rearrange("p (a r) -> p a r", r=P)[:, :, 0:rows]).then_inc(h_hi_done, 1)

            def split(b, i, first):
                loaded, blk = (g_loaded, u_loaded)[i % 2], b + i // 4
                act.wait_ge(loaded, 16 * blk + 16)
                if not first or i >= 2:
                    act.wait_ge(tile_done, 4 * b + i - 1)
                nc.scalar.copy(w_hi[i % 2][:, :, :], raw_of(i)).then_inc(w_hi_done, 1)

            def silu(b, f):
                act.wait_ge(tile_done, 4 * b + 2 * f + 1)
                if f == 1:
                    act.wait_ge(prod_done, 2 * b + 1)
                nc.scalar.activation(gated[:, :].rearrange("p (c r) -> p c r", c=NCH), pg[:, :, 0:TC], ACT.Silu)\
                    .then_inc(silu_done, 1)

            def act_hi(b, f, first):
                act.wait_ge(prod_done, 2 * b + f + 1)
                if not first and f == 0:
                    act.wait_ge(piece_done, b * NU)
                nc.scalar.copy(a_hi[:, f, :], prod[:, :]).then_inc(a_hi_done, 1)

            split(0, 0, True)

            def body(b, first, last):
                split(b, 1, first)
                if not first:
                    act.wait_ge(prod_done, 2 * b)
                silu(b, 0)
                split(b, 2, first)
                act.wait_ge(d_loaded, 16 * b + 16)
                if not first:
                    act.wait_ge(piece_done, b * NU)
                nc.scalar.copy(d_hi[:, :, :], d_raw[:, :, :]).then_inc(d_hi_done, 1)
                act_hi(b, 0, first)
                split(b, 3, first)
                silu(b, 1)
                if not last:
                    split(b, 4, first)
                act_hi(b, 1, first)

            blocks(act, body)

        @block.gpsimd
        def _(pool):
            norm.power_first()

            def split(b, i):
                pool.wait_ge(w_hi_done, 4 * b + i + 1)
                nc.gpsimd.tensor_tensor(w_lo[i % 2][:, :, :], raw_of(i), f32(w_hi[i % 2][:, :, :]), ALU.subtract)\
                    .then_inc(w_lo_done, 1)

            split(0, 0)

            def body(b, first, last):
                split(b, 1)
                split(b, 2)
                pool.wait_ge(d_hi_done, b + 1)
                nc.gpsimd.tensor_tensor(d_lo[:, :, :], d_raw[:, :, :], f32(d_hi[:, :, :]), ALU.subtract)\
                    .then_inc(d_lo_done, 1)
                split(b, 3)
                if not last:
                    split(b, 4)

            blocks(pool, body)

            def shift_rows(t):
                rows = TILES[t][2]
                pool.wait_ge(scaled_done, t + 1)
                nc.gpsimd.tensor_tensor(y[0:rows, t, :], y[0:rows, t, :], shift[0:rows, :], ALU.add)\
                    .then_inc(shifted, 1)

            for t, r0, rows in TILES:
                norm.root(pool, t, rows)
                if t >= 1:
                    shift_rows(t - 1)
            shift_rows(NT)

        @block.vector
        def _(dve):
            for q in range(2 * (NT + 1)):
                t, half = q // 2, q % 2
                _, r0, rows = TILES[t]
                dve.wait_ge(h_hi_done, q + 1)
                nc.vector.tensor_tensor(h_lo[:, 4 * half:4 * half + 4, r0:r0 + rows],
                                        hT_banks[q % 4].rearrange("p (a r) -> p a r", r=P)[:, :, 0:rows],
                                        f32(h_hi[:, 4 * half:4 * half + 4, r0:r0 + rows]), ALU.subtract)\
                    .then_inc(h_lo_done, 1)
                if half == 1:
                    nc.vector.tensor_scalar(y[0:rows, t, :], y[0:rows, t, :], ALPHA, None, ALU.mult)\
                        .then_inc(y_ready, 1)
            dve.wait_ge(y_ready, NT + 1)

            def body(b, first, last):
                for f in range(2):
                    dve.wait_ge(silu_done, 2 * b + f + 1)
                    dve.wait_ge(tile_done, 4 * b + 2 * f + 2)
                    if not first or f >= 1:
                        dve.wait_ge(a_lo_done, 2 * b + f)
                    nc.vector.tensor_tensor(prod[:, :].rearrange("p (c r) -> p c r", c=NCH),
                                            gated[:, :].rearrange("p (c r) -> p c r", c=NCH), pu[:, :, 0:TC], ALU.mult)\
                        .then_inc(prod_done, 1)
                    dve.wait_ge(a_hi_done, 2 * b + f + 1)
                    nc.vector.tensor_tensor(a_lo[:, f, :], prod[:, :], f32(a_hi[:, f, :]), ALU.subtract)\
                        .then_inc(a_lo_done, 1)

                def scale_rows(t):
                    rows = TILES[t][2]
                    norm.scaled(dve, t, rows, y[0:rows, t, :]).then_inc(scaled_done, 1)

                for i in range(NU):
                    t, half = i // 2, i % 2
                    rows = TILES[t][2]
                    o = y[0:rows, t, 512 * half:512 * half + 512]
                    dve.wait_ge(piece_done, b * NU + i + 1)
                    nc.vector.tensor_tensor(o, o, pd[0:rows, i % 2, :], ALU.add).then_inc(added, 1)
                    if last and half == 1:
                        dve.wait_ge(added, b * NU + i + 1)
                        norm.moments(dve, t, rows, y[0:rows, t, :])
                        if t >= 1:
                            scale_rows(t - 1)
                if last:
                    scale_rows(NT)

            blocks(dve, body)


_OUTS = {"y": (ROWS, D), "fkT": (FOX_H * HD, ROWS), "fv": (ROWS, FOX_H * HD), "logf": (ROWS, FOX_H),
         "dk": (ROWS, KV_H * HD), "dv": (ROWS, KV_H * HD), "ik": (ROWS, HD)}
_SCRATCH = {"dq": (ROWS, DSA_H * HD), "negc": (FOX_H, SEQ), "bias_s": (FOX_H, KEYS_S)}


def kernel(**inputs):
    import numpy as np
    import concourse.bacc as bacc
    from concourse.bass_utils import run_bass_kernel_spmd as run

    i = {k: np.asarray(v) for k, v in inputs.items()}
    x = np.concatenate([i["x_prompt"][0], i["x_sample"][0]], 0)
    inv = np.float32(5e5) ** (-np.arange(HALF, dtype=np.float32) * np.float32(2.0) / np.float32(ROT))
    ang = np.zeros(((NT + 1) * P, HALF), np.float32)
    ang[:ROWS] = np.arange(ROWS, dtype=np.float32)[:, None] * inv[None, :].astype(np.float32)
    tiled = lambda a: np.ascontiguousarray(a.astype(np.float32).reshape(NT + 1, P, HALF).transpose(1, 0, 2))
    arrays = {
        "x": x, "xT": x.T, "cos": tiled(np.cos(ang)), "sin": tiled(np.sin(ang)),
        "w_in": i["w_in"][0], "b_forget": i["b_forget"][0], "w_out": i["w_out"][0],
        "ln1_g": i["ln1_g"][0], "ln1_b": i["ln1_b"][0], "ln2_g": i["ln2_g"][0], "ln2_b": i["ln2_b"][0],
        "w_gate": i["w_gate"][0], "w_up": i["w_up"][0], "w_down": i["w_down"][0],
        "past_fkT": i["cache_fox_k"][0, 0].reshape(PAST, -1).T, "past_fv": i["cache_fox_v"][0, 0].reshape(PAST, -1),
        "past_logfT": i["cache_fox_logf"][0, 0].T, "past_dkT": i["cache_dsa_k"][0, 0].reshape(PAST, -1).T,
        "past_dv": i["cache_dsa_v"][0, 0].reshape(PAST, -1), "past_ikT": i["cache_idx_k"][0, 0].T,
    }
    arrays = {k: np.ascontiguousarray(v) for k, v in arrays.items()}
    nc = bacc.Bacc("TRN2", target_bir_lowering=False, num_devices=1)
    d = {k: nc.dram_tensor("in_" + k, v.shape, mybir.dt.from_np(v.dtype), kind="ExternalInput").ap()
         for k, v in arrays.items()}
    for k, shape in _OUTS.items():
        d[k] = nc.dram_tensor("out_" + k, shape, F32, kind="ExternalOutput").ap()
    for k, shape in _SCRATCH.items():
        d[k] = nc.dram_tensor("scratch_" + k, shape, F32, kind="Internal").ap()
    build(nc, d)
    r = run(nc, [{"in_" + k: v for k, v in arrays.items()}], core_ids=[0]).results[0]
    y, fkT, fv, logf, dk, dv, ik = (r["out_" + k] for k in _OUTS)
    fk = fkT.T

    def states(s):
        n = s.stop - s.start
        return (fk[s].reshape(1, 1, n, FOX_H, HD), fv[s].reshape(1, 1, n, FOX_H, HD), logf[s].reshape(1, 1, n, FOX_H),
                dk[s].reshape(1, 1, n, KV_H, HD), dv[s].reshape(1, 1, n, KV_H, HD), ik[s].reshape(1, 1, n, HD))

    p, s = slice(0, SEQ), slice(SEQ, ROWS)
    return (y[p][None], y[s][None], *states(p), *states(s))
```

```python
import concourse.bass as bass
from concourse import mybir

F32 = mybir.dt.float32
F32R = mybir.dt.float32r
BF16 = mybir.dt.bfloat16
FP16 = mybir.dt.float16
I32 = mybir.dt.int32
I16 = mybir.dt.int16
U16 = mybir.dt.uint16
ALU = mybir.AluOpType
ACT = mybir.ActivationFunctionType

P = 128
D = 1024
KD = D // P
SEQ, NEW, PAST = 1024, 32, 1024
ROWS = SEQ + NEW
NT = SEQ // P
TILES = [(t, t * P, P) for t in range(NT)] + [(NT, SEQ, NEW)]
KEYS_S = PAST + NEW
HD = 64
FOX_H, DSA_H, KV_H, IDX_H = 8, 8, 2, 4
ROT = HD // 4
HALF = ROT // 2
CHUNK = 64
TOPK = 256
D_FF = -(-8 * D // (3 * 256)) * 256
ALPHA = 2.0 ** 0.25
LN_EPS = 1e-5
SCALE = HD ** -0.5
BIG = 1e30
LOWEST = -3e38

C_FQ, C_FK, C_FV = 0, 512, 1024
C_FF = 1536
C_DQ = C_FF + FOX_H
C_DK = C_DQ + DSA_H * HD
C_DV = C_DK + KV_H * HD
C_IQ = C_DV + KV_H * HD
C_IK = C_IQ + IDX_H * HD
C_IW = C_IK + HD
IN_WIDTH = C_IW + IDX_H

TC = ROWS // 3
NCH = 3

SEG = []
_at = 0
for _t in range(TOPK // P, NT):
    SEG.append((_t, _at, P, (_t + 1) * P))
    _at += (_t + 1) * P
SEG.append((NT, _at, NEW, KEYS_S))
SCORES = _at + KEYS_S
NSEG = len(SEG)
SETS = [slice(0, 4), slice(4, NSEG)]


def f32(ap):
    return ap.bitcast(F32)


class Places:

    def __init__(self, nc, start, end):
        self.nc, self.at, self.end = nc, start, end

    def __call__(self, name, shape, dt):
        n = 2 if dt in (BF16, FP16) else 4
        for s in shape[1:]:
            n *= s
        t = self.nc.alloc_sbuf_tensor_at(name, shape, dt, offset=self.at)
        self.at += -(-n // 32) * 32
        assert self.at <= self.end, (name, self.at - self.end)
        return t


def build(nc, d):
    base = -(-nc.sbuf_base // 64) * 64
    end = nc.sbuf_usable_end
    t_size = 2 * 2 * 4 * ROWS * 4
    keep = Places(nc, base, end)
    c = {}
    c["score"] = keep("score", [P, SCORES], F32)
    c["ident"] = keep("ident", [P, P], F32)
    c["ident16"] = keep("ident16", [P, P], BF16)
    c["causal16"] = keep("causal16", [P, P], BF16)
    c["corner"] = keep("corner", [P, 2 * P], F32)
    c["causal_s16"] = keep("causal_s16", [P, NEW], BF16)
    c["logf"] = keep("logf", [P, NT + 1, FOX_H], F32)
    tr = keep.at
    c["t_region"] = tr
    rest = tr + t_size
    c["rest"] = rest
    c["end"] = end
    tp = Places(nc, tr, rest)
    c["kT_hi"] = tp("fox_kT_hi", [P, 4, ROWS], F32R)
    c["kT_lo"] = tp("fox_kT_lo", [P, 4, ROWS], F32R)
    c["qT_hi"] = tp("fox_qT_hi", [P, 4, ROWS], F32R)
    c["qT_lo"] = tp("fox_qT_lo", [P, 4, ROWS], F32R)
    rp = Places(nc, rest, end)
    c["mix"] = rp("mix", [P, NT + 1, D], F32)
    c["after_mix"] = rp.at
    project(nc, d, c)
    fox(nc, d, c)
    dsa(nc, d, c)
    mix_out(nc, d, c)
    ffn(nc, d, c)



IX = (IDX_H + 1) * HD

GROUPS = [("ix", [(C_IQ, IX + IDX_H), (C_FF, FOX_H)], False),
          ("dq", [(C_DQ, 256)], False), ("fv", [(C_FV, 256)], False),
          ("dq", [(C_DQ + 256, 256)], False), ("fv", [(C_FV + 256, 256)], False),
          ("dkv", [(C_DK, 256)], False),
          ("fk", [(C_FK, 256)], True), ("fk", [(C_FK + 256, 256)], True),
          ("fq", [(C_FQ, 256)], True), ("fq", [(C_FQ + 256, 256)], True)]
NG = len(GROUPS)
FK = [g[0] for g in GROUPS].index("fk")
PARTS = 8
IX_GAP = 3


def width(g):
    return sum(n for _, n in GROUPS[g][1])


UNITS = []
for _g, (_name, _, _tr) in enumerate(GROUPS):
    if _tr:
        UNITS += [(_g, _m, _c) for _m in range(2) for _c in range(NCH)]
    else:
        UNITS += [(_g, _t, None) for _t in range(NT + 1)]
OF_GROUP = [[u for u, x in enumerate(UNITS) if x[0] == g] for g in range(NG)]
ROPED = [u for u, x in enumerate(UNITS) if GROUPS[x[0]][0] in ("ix", "dq", "dkv")]
STAGED = [u for u, x in enumerate(UNITS) if GROUPS[x[0]][0] in ("dq", "dkv", "fv")]
TRANS = [u for u, x in enumerate(UNITS) if GROUPS[x[0]][2]]
NSTAGE = 3


def project(nc, d, c):
    from contextlib import ExitStack
    with ExitStack() as ctx:
        def sem(name):
            return ctx.enter_context(nc.semaphore(name))

        tr, rest, end = c["t_region"], c["rest"], c["end"]
        pl = Places(nc, rest, end)
        x_hi = pl("x_hi", [P, KD, ROWS], F32R)
        x_lo = pl("x_lo", [P, KD, ROWS], F32R)
        w_hi = [pl(f"w_hi{s}", [P, KD, 256], F32R) for s in range(2)]
        w_lo = [pl(f"w_lo{s}", [P, KD, 256], F32R) for s in range(2)]
        w_raw = pl("w_raw", [P, KD, 256], F32)
        half = tr + (rest - tr) // 2
        a = Places(nc, tr, half)
        x_raw = a("x_raw", [P, KD, ROWS], F32)
        a = Places(nc, tr, half)
        ix_row = a("ix_row", [P, NT + 1, IX + HD], F32)
        relu = [a(f"relu{s}", [P, KEYS_S], F32) for s in range(2)]
        past_ik = a("past_ik", [P, PAST], F32)
        b = Places(nc, half, rest)
        iT_hi = b("iT_hi", [P, 3, ROWS], F32R)
        iT_lo = b("iT_lo", [P, 3, ROWS], F32R)
        iT_new = b("iT_new", [P, 3, NEW], F32)
        b = Places(nc, half, rest)
        w0_raw = b("w0_raw", [P, KD, width(0)], F32)
        w0_hi = b("w0_hi", [P, KD, width(0)], F32R)
        w0_lo = b("w0_lo", [P, KD, width(0)], F32R)
        stage = [pl(f"stage{s}", [P, 256], F32) for s in range(NSTAGE)]
        tstage = [pl(f"tstage{s}", [P, TC], F32) for s in range(2)]
        iwff = pl("iwff", [P, NT + 1, IDX_H + FOX_H], F32)
        zf = pl("zf", [P, NT + 1, FOX_H], F32)
        az = pl("az", [P, NT + 1, FOX_H], F32)
        lz = pl("lz", [P, NT + 1, FOX_H], F32)
        bf = pl("b_forget_rows", [P, FOX_H], F32)
        cos = pl("cos", [P, NT + 1, HALF], F32)
        sin = pl("sin", [P, NT + 1, HALF], F32)
        ra = pl("rope_a", [P, IDX_H + 1, HALF], F32)
        rb = pl("rope_b", [P, IDX_H + 1, HALF], F32)
        rc = pl("rope_c", [P, IDX_H + 1, HALF], F32)
        rd = pl("rope_d", [P, IDX_H + 1, HALF], F32)
        key_buf = pl("key_buf", [P, KEYS_S], I32)
        cnt = pl("cnt", [P, NSEG], F32)
        want = pl("want", [P, NSEG], F32)
        reached = pl("reached", [P, NSEG], F32)
        low = pl("low", [P, NSEG], F32)
        candidate = pl("candidate", [P, NSEG], F32)
        top_key = pl("top_key", [P, NSEG], F32)
        bit = pl("bit", [P, 2], F32)
        score, ident = c["score"], c["ident"]

        pj = ctx.enter_context(nc.psum_tensor("pj", [P, 2, 512], F32))
        pi = ctx.enter_context(nc.psum_tensor("pi", [P, 6 * 512], F32))

        x_loaded = [sem(f"x_loaded{k}") for k in range(KD)]
        x_hi_done, x_lo_done = sem("x_hi_done"), sem("x_lo_done")
        w0_loaded, w_loaded, w_hi_done, w_lo_done = sem("w0_loaded"), sem("w_loaded"), sem("w_hi_done"), sem("w_lo_done")
        unit_done, unit_out = sem("unit_done"), sem("unit_out")
        roped = sem("roped")
        t_lo_done = sem("t_lo_done")
        stage_free = [sem(f"stage_free{s}") for s in range(NSTAGE)]
        tstage_free = [sem(f"tstage_free{s}") for s in range(2)]
        small_loaded, past_loaded = sem("small_loaded"), sem("past_loaded")
        consts, rope_step = sem("consts"), sem("rope_step")
        i_tr, i_hi, i_lo, i_new = sem("i_tr"), sem("i_hi"), sem("i_lo"), sem("i_new")
        i_qk, i_relu, i_sum = sem("i_qk"), sem("i_relu"), sem("i_sum")
        z_done, l_done, logf_done = sem("z_done"), sem("l_done"), sem("logf_done")
        step = sem("step")
        key_done, planes_done = sem("key_done"), sem("planes_done")
        bank_step = sem("rows_out")
        block = ctx.enter_context(nc.Block())

        x_rows = d["xT"].rearrange("(k p) n -> k p n", p=P)
        w_cols = d["w_in"].rearrange("(k p) n -> p k n", p=P)

        def weights(g):
            return (w0_raw, w0_hi, w0_lo) if g == 0 else (w_raw, w_hi[g % 2], w_lo[g % 2])

        def hi_plane(j):
            _, at, rows, L = SEG[j]
            return score[0:rows, at:at + L].bitcast(I16)[:, 0:L]

        def lo_plane(j):
            _, at, rows, L = SEG[j]
            return score[0:rows, at:at + L].bitcast(U16)[:, L:2 * L]

        def flags(j):
            at = (j % 2) * KEYS_S
            return key_buf[0:SEG[j][2], :].bitcast(BF16)[:, at:at + SEG[j][3]]

        def ranks(j):
            return pi[0:SEG[j][2], 1536 * (j % 2):1536 * (j % 2) + SEG[j][3]]

        def loads_of(g):
            return 16 * sum(len(GROUPS[i][1]) for i in range(1, g + 1))

        def stage_value(i):
            return sum(32 if GROUPS[UNITS[STAGED[j]][0]][0] == "dkv" else 16
                       for j in range(i % NSTAGE, i + 1, NSTAGE))

        IDX = [(j, h) for j in range(NSEG) for h in range(IDX_H)]
        last = OF_GROUP[1][IX_GAP]
        BEFORE, BETWEEN = range(last), last
        PIECES = range(len(IDX) // PARTS * PARTS)
        FILLERS = range(last + 1, last + 1 + len(IDX) // PARTS)
        AFTER = range(FILLERS[-1] + 1, len(UNITS))

        @block.sync
        def _(sp):
            def load_w(g):
                if g >= 2:
                    sp.wait_ge(w_hi_done, g)
                    sp.wait_ge(w_lo_done, g)
                at = 0
                for c0, n in GROUPS[g][1]:
                    sp.dma_start(weights(g)[0][:, :, at:at + n], w_cols[:, :, c0:c0 + n])\
                        .then_inc(w0_loaded if g == 0 else w_loaded, 16)
                    at += n

            load_w(0)
            for k in range(KD):
                sp.dma_start(x_raw[:, k, :], x_rows[k]).then_inc(x_loaded[k], 16)
            sp.dma_start(cos[:, :, :], d["cos"]).then_inc(small_loaded, 16)
            sp.dma_start(sin[:, :, :], d["sin"]).then_inc(small_loaded, 16)
            sp.dma_start(bf[:, :], d["b_forget"].partition_broadcast(P)).then_inc(small_loaded, 16)
            load_w(1)
            sp.wait_ge(x_lo_done, KD)
            for r in range(2):
                sp.dma_start(past_ik[r * HD:(r + 1) * HD, :], d["past_ikT"]).then_inc(past_loaded, 16)
            n_out = 0
            for g in range(NG):
                name = GROUPS[g][0]
                if g + 2 < NG:
                    load_w(g + 2)
                for u in OF_GROUP[g]:
                    _, t, ch = UNITS[u]
                    if GROUPS[g][2]:
                        i = TRANS.index(u)
                        if name == "fk":
                            sp.wait_ge(unit_out, u + 1)
                            f0 = (g - FK) * 256 + t * P
                            sp.dma_start(d["fkT"][f0:f0 + P, ch * TC:(ch + 1) * TC],
                                         tstage[i % 2][:, :]).then_inc(tstage_free[i % 2], 16)
                        continue
                    _, r0, rows = TILES[t]
                    if u in ROPED:
                        sp.wait_ge(roped, ROPED.index(u) + 1)
                    else:
                        sp.wait_ge(unit_out, u + 1)
                    if name == "ix":
                        sp.dma_start(d["ik"][r0:r0 + rows, :], ix_row[0:rows, t, IX - HD:IX]).then_inc(bank_step, 16)
                        n_out += 16
                    if u not in STAGED:
                        continue
                    i = STAGED.index(u)
                    s = stage[i % NSTAGE]
                    if name == "dkv":
                        sp.dma_start(d["dk"][r0:r0 + rows, :], s[0:rows, 0:P]).then_inc(stage_free[i % NSTAGE], 16)
                        sp.dma_start(d["dv"][r0:r0 + rows, :], s[0:rows, P:2 * P]).then_inc(stage_free[i % NSTAGE], 16)
                    else:
                        c0 = GROUPS[g][1][0][0] - (C_DQ if name == "dq" else C_FV)
                        sp.dma_start(d[name][r0:r0 + rows, c0:c0 + 256], s[0:rows, :]).then_inc(stage_free[i % NSTAGE], 16)
                if g == 2:
                    sp.wait_ge(logf_done, 1)
                    sp.dma_start(d["logf"][0:SEQ, :].rearrange("(t p) h -> p t h", p=P),
                                 c["logf"][:, 0:NT, :]).then_inc(bank_step, 16)
                    sp.dma_start(d["logf"][SEQ:ROWS, :], c["logf"][0:NEW, NT, :]).then_inc(bank_step, 16)
                    n_out += 32
            sp.wait_ge(bank_step, n_out)
            for s in range(NSTAGE):
                last = max(i for i in range(len(STAGED)) if i % NSTAGE == s)
                sp.wait_ge(stage_free[s], stage_value(last))
            nk = len(OF_GROUP[FK]) + len(OF_GROUP[FK + 1])
            for s in range(2):
                sp.wait_ge(tstage_free[s], 16 * (nk // 2))

        @block.scalar
        def _(act):
            def split_w(g):
                n = width(g)
                if g == 0:
                    act.wait_ge(w0_loaded, 16 * len(GROUPS[0][1]))
                else:
                    act.wait_ge(w_loaded, loads_of(g))
                if g >= 3:
                    act.wait_ge(unit_done, OF_GROUP[g - 2][-1] + 1)
                raw, hi, _ = weights(g)
                nc.scalar.copy(hi[:, :, 0:n], raw[:, :, 0:n]).then_inc(w_hi_done, 1)

            def copy_out(u):
                g, t, ch = UNITS[u]
                name = GROUPS[g][0]
                act.wait_ge(unit_done, u + 1)
                if GROUPS[g][2]:
                    i = TRANS.index(u)
                    if i == 0:
                        act.wait_ge(i_sum, len(IDX))
                    if i >= 2:
                        act.wait_ge(t_lo_done, i - 1)
                        if i - 2 < 12:
                            act.wait_ge(tstage_free[i % 2], 16 * ((i - 2) // 2 + 1))
                    hi = c["kT_hi"] if name == "fk" else c["qT_hi"]
                    m = 2 * ((g - FK) % 2) + t
                    sc = 1.0 if name == "fk" else SCALE
                    nc.scalar.activation(tstage[i % 2][:, :], pj[:, u % 2, 0:TC], ACT.Copy, scale=sc)
                    nc.scalar.activation(hi[:, m, ch * TC:(ch + 1) * TC], pj[:, u % 2, 0:TC], ACT.Copy,
                                         scale=sc).then_inc(unit_out, 1)
                    return
                rows = TILES[t][2]
                if name == "ix":
                    if t == 0:
                        act.wait_ge(consts, 5)
                    nc.scalar.copy(iwff[0:rows, t, :], pj[0:rows, u % 2, IX:IX + IDX_H + FOX_H])
                    dst, n = ix_row[0:rows, t, 0:IX], IX
                else:
                    i = STAGED.index(u)
                    if i >= NSTAGE:
                        act.wait_ge(stage_free[i % NSTAGE], stage_value(i - NSTAGE))
                    dst, n = stage[i % NSTAGE][0:rows, :], 256
                nc.scalar.copy(dst, pj[0:rows, u % 2, 0:n]).then_inc(unit_out, 1)

            def index_hi():
                for t, r0, rows in TILES:
                    act.wait_ge(i_tr, t + 1)
                    src = pi[:, (t % 6) * 512:(t % 6) * 512 + 3 * P].rearrange("p (a r) -> p a r", a=3)
                    nc.scalar.copy(iT_hi[:, :, r0:r0 + rows], src[:, :, 0:rows]).then_inc(i_hi, 1)

            def planes(j):
                rows, L = SEG[j][2:]
                act.wait_ge(key_done, j + 1)
                halves = key_buf[0:rows, 0:L]
                nc.scalar.copy(hi_plane(j), halves.bitcast(I16)[:, 1:2 * L:2])
                nc.scalar.copy(lo_plane(j), halves.bitcast(U16)[:, 0:2 * L:2]).then_inc(planes_done, 1)

            def index_relu():
                act.wait_ge(z_done, 1)
                nc.scalar.activation(az[:, :, :], az[:, :, :], ACT.Exp, scale=-1.0).then_inc(l_done, 1)
                act.wait_ge(l_done, 1)
                nc.scalar.activation(lz[:, :, :], az[:, :, :], ACT.Ln, bias=1.0).then_inc(l_done, 1)
                for n, (j, h) in enumerate(IDX):
                    _, _, rows, L = SEG[j]
                    act.wait_ge(i_qk, n + 1)
                    if n >= 2:
                        act.wait_ge(i_sum, n - 1)
                    o = 1536 * (n % 2)
                    nc.scalar.activation(relu[n % 2][0:rows, 0:L], pi[0:rows, o:o + L], ACT.Relu)\
                        .then_inc(i_relu, 1)
                    if n in PIECES[PARTS - 1::PARTS]:
                        take(FILLERS[n // PARTS])
                    if h == 1 and j >= 1:
                        planes(j - 1)
                planes(NSEG - 1)

            split_w(0)
            for k in range(KD):
                act.wait_ge(x_loaded[k], 16)
                nc.scalar.copy(x_hi[:, k, :], x_raw[:, k, :]).then_inc(x_hi_done, 1)
            split_w(1)
            act.wait_ge(x_lo_done, KD)

            def take(u):
                g = UNITS[u][0]
                if u == OF_GROUP[g][0] and 1 <= g < NG - 1:
                    split_w(g + 1)
                copy_out(u)

            for u in BEFORE:
                take(u)
            index_hi()
            take(BETWEEN)
            index_relu()
            for u in AFTER:
                take(u)

        @block.gpsimd
        def _(pool):
            ident16, causal16, corner = c["ident16"], c["causal16"], c["corner"]
            nc.gpsimd.memset(ident[:, :], 0.0).then_inc(rope_step, 1)
            nc.gpsimd.memset(causal16[:, :], 0.0).then_inc(rope_step, 1)
            pool.wait_ge(rope_step, 2)
            nc.gpsimd.affine_select(out=ident[:, :], in_=ident[:, :], compare_op=ALU.not_equal, fill=1.0,
                                    base=0, pattern=[[-1, P]], channel_multiplier=1).then_inc(consts, 1)
            nc.gpsimd.affine_select(out=causal16[:, :], in_=causal16[:, :], compare_op=ALU.is_ge, fill=-BIG,
                                    base=0, pattern=[[-1, P]], channel_multiplier=1).then_inc(consts, 1)
            pool.wait_ge(consts, 2)
            nc.gpsimd.tensor_copy(ident16[:, :], ident[:, :]).then_inc(consts, 1)
            nc.gpsimd.memset(corner[:, :], 0.0).then_inc(rope_step, 1)
            nc.gpsimd.memset(iwff[:, :, :], 0.0).then_inc(consts, 1)
            pool.wait_ge(rope_step, 3)
            nc.gpsimd.memset(corner[0:CHUNK, 2 * P - CHUNK:2 * P], -BIG).then_inc(consts, 1)
            steps = [3]

            def split_w(g):
                n = width(g)
                pool.wait_ge(w_hi_done, g + 1)
                raw, hi, lo = weights(g)
                nc.gpsimd.tensor_tensor(lo[:, :, 0:n], raw[:, :, 0:n], f32(hi[:, :, 0:n]), ALU.subtract)\
                    .then_inc(w_lo_done, 1)

            def rope(view, t, rows, heads):
                x1, x2 = view[:, :, 0:HALF], view[:, :, HALF:ROT]
                co = cos[0:rows, t, :].unsqueeze(1).broadcast_to((rows, heads, HALF))
                si = sin[0:rows, t, :].unsqueeze(1).broadcast_to((rows, heads, HALF))
                for out, x, y in ((ra, x1, co), (rb, x2, si), (rc, x2, co), (rd, x1, si)):
                    nc.gpsimd.tensor_tensor(out[0:rows, 0:heads, :], x, y, ALU.mult).then_inc(rope_step, 1)
                steps[0] += 4
                pool.wait_ge(rope_step, steps[0])
                nc.gpsimd.tensor_tensor(x1, ra[0:rows, 0:heads, :], rb[0:rows, 0:heads, :], ALU.subtract)\
                    .then_inc(rope_step, 1)
                steps[0] += 1
                return nc.gpsimd.tensor_tensor(x2, rc[0:rows, 0:heads, :], rd[0:rows, 0:heads, :], ALU.add)

            split_w(1)
            pool.wait_ge(small_loaded, 48)
            for g in range(NG):
                if 1 <= g < NG - 1:
                    split_w(g + 1)
                name = GROUPS[g][0]
                for u in OF_GROUP[g]:
                    _, t, ch = UNITS[u]
                    if GROUPS[g][2]:
                        i = TRANS.index(u)
                        pool.wait_ge(unit_out, u + 1)
                        hi, lo = (c["kT_hi"], c["kT_lo"]) if name == "fk" else (c["qT_hi"], c["qT_lo"])
                        m = 2 * ((g - FK) % 2) + t
                        nc.gpsimd.tensor_tensor(lo[:, m, ch * TC:(ch + 1) * TC], tstage[i % 2][:, :],
                                                f32(hi[:, m, ch * TC:(ch + 1) * TC]), ALU.subtract)\
                            .then_inc(t_lo_done, 1)
                        continue
                    if u not in ROPED:
                        continue
                    rows = TILES[t][2]
                    pool.wait_ge(unit_out, u + 1)
                    if name == "ix":
                        view, heads = ix_row[0:rows, t, 0:IX].rearrange("p (h e) -> p h e", e=HD), IDX_H + 1
                    elif name == "dq":
                        view = stage[STAGED.index(u) % NSTAGE][0:rows, :].rearrange("p (h e) -> p h e", e=HD)
                        heads = 4
                    else:
                        view = stage[STAGED.index(u) % NSTAGE][0:rows, 0:P].rearrange("p (h e) -> p h e", e=HD)
                        heads = KV_H
                    last = rope(view, t, rows, heads)
                    if name == "ix":
                        last.then_inc(rope_step, 1)
                        steps[0] += 1
                        pool.wait_ge(rope_step, steps[0])
                        last = nc.gpsimd.tensor_copy(ix_row[0:rows, t, IX:IX + HD], ix_row[0:rows, t, IX - HD:IX])
                    last.then_inc(roped, 1)
                    pool.wait_ge(rope_step, steps[0])
                    pool.wait_ge(roped, ROPED.index(u) + 1)

        @block.tensor
        def _(pe):
            def unit(u, ks=range(KD)):
                g, t, ch = UNITS[u]
                n = width(g)
                _, hi, lo = weights(g)
                if ks[0] == 0:
                    if u == OF_GROUP[g][0]:
                        pe.wait_ge(w_lo_done, g + 1)
                    if u >= 2:
                        pe.wait_ge(unit_out, u - 1)
                for k in ks:
                    if u == 0:
                        pe.wait_ge(x_lo_done, k + 1)
                    if GROUPS[g][2]:
                        out = pj[:, u % 2, 0:TC]
                        cols, rows = slice(t * P, (t + 1) * P), slice(ch * TC, (ch + 1) * TC)
                        pairs = [(hi[:, k, cols], x_hi[:, k, rows]), (hi[:, k, cols], x_lo[:, k, rows]),
                                 (lo[:, k, cols], x_hi[:, k, rows])]
                    else:
                        _, r0, nr = TILES[t]
                        out = pj[0:nr, u % 2, 0:n]
                        xh, xl = x_hi[:, k, r0:r0 + nr], x_lo[:, k, r0:r0 + nr]
                        pairs = [(xh, hi[:, k, 0:n]), (xh, lo[:, k, 0:n]), (xl, hi[:, k, 0:n])]
                    for i, (l, r) in enumerate(pairs):
                        mm = nc.tensor.matmul(out, l, r, start=(k == 0 and i == 0), stop=(k == KD - 1 and i == 2))
                if ks[-1] == KD - 1:
                    mm.then_inc(unit_done, 1)

            def index_transposes():
                pe.wait_ge(consts, 5)
                for t, r0, rows in TILES:
                    pe.wait_ge(roped, t + 1)
                    if t >= 6:
                        pe.wait_ge(i_lo, t - 5)
                    o = (t % 6) * 512
                    for a_ in range(3):
                        mm = nc.tensor.transpose(pi[:, o + a_ * P:o + a_ * P + rows],
                                                 ix_row[0:rows, t, a_ * P:(a_ + 1) * P], ident[0:rows, 0:rows])
                    mm.then_inc(i_tr, 1)

            def index_scores():
                pe.wait_ge(i_lo, NT + 1)
                pe.wait_ge(i_new, 1)
                pe.wait_ge(past_loaded, 32)
                for n, (j, h) in enumerate(IDX):
                    t, _, rows, L = SEG[j]
                    if n >= 2:
                        pe.wait_ge(i_relu, n - 1)
                    o = 1536 * (n % 2)
                    part, q = slice(HD * (h % 2), HD * (h % 2) + HD), h // 2
                    if t < NT:
                        qs = slice(t * P, t * P + P)
                        for k0 in range(0, L, 512):
                            ks = slice(k0, min(L, k0 + 512))
                            out = pi[:, o + ks.start:o + ks.stop]
                            nc.tensor.matmul(out, iT_hi[part, q, qs], iT_hi[part, 2, ks], start=True, stop=False)
                            nc.tensor.matmul(out, iT_hi[part, q, qs], iT_lo[part, 2, ks], start=False, stop=False)
                            mm = nc.tensor.matmul(out, iT_lo[part, q, qs], iT_hi[part, 2, ks], start=False, stop=True)
                    else:
                        for k0 in range(0, PAST, 512):
                            nc.tensor.matmul(pi[0:NEW, o + k0:o + k0 + 512], iT_new[part, q, :],
                                             past_ik[part, k0:k0 + 512], start=True, stop=True)
                        mm = nc.tensor.matmul(pi[0:NEW, o + PAST:o + KEYS_S], iT_new[part, q, :],
                                              iT_new[part, 2, :], start=True, stop=True)
                    mm.then_inc(i_qk, 1)
                    if n in PIECES:
                        unit(FILLERS[n // PARTS], range(KD)[n % PARTS * KD // PARTS:(n % PARTS + 1) * KD // PARTS])

            for u in BEFORE:
                unit(u)
            index_transposes()
            unit(BETWEEN)
            index_scores()
            for u in AFTER:
                unit(u)

        @block.vector
        def _(dve):
            def key_of(j):
                t, at, rows, L = SEG[j]
                bits, k = score[0:rows, at:at + L].bitcast(I32), key_buf[0:rows, 0:L]
                if j >= 1:
                    dve.wait_ge(planes_done, j)
                did(nc.vector.tensor_scalar(k, bits, 31, 2 ** 31 - 1, ALU.arith_shift_right, ALU.bitwise_and))
                settled()
                nc.vector.tensor_tensor(k, k, bits, ALU.bitwise_xor).then_inc(key_done, 1)

            n = [0]

            def did(ins):
                n[0] += 1
                ins.then_inc(step, 1)

            def settled():
                dve.wait_ge(step, n[0])

            dve.wait_ge(w_hi_done, 1)
            nc.vector.tensor_tensor(w0_lo[:, :, :], w0_raw[:, :, :], f32(w0_hi[:, :, :]), ALU.subtract)\
                .then_inc(w_lo_done, 1)
            for k in range(KD):
                dve.wait_ge(x_hi_done, k + 1)
                nc.vector.tensor_tensor(x_lo[:, k, :], x_raw[:, k, :], f32(x_hi[:, k, :]), ALU.subtract)\
                    .then_inc(x_lo_done, 1)
            did(nc.vector.memset(cnt[:, :], 0.0))
            did(nc.vector.memset(want[:, :], float(TOPK)))
            dve.wait_ge(consts, 2)
            for j in range(4):
                did(nc.vector.tensor_copy(c["causal_s16"][j * NEW:(j + 1) * NEW, :], c["causal16"][0:NEW, 0:NEW]))
            dve.wait_ge(small_loaded, 48)
            dve.wait_ge(unit_out, OF_GROUP[0][-1] + 1)
            did(nc.vector.tensor_tensor(zf[:, :, :], iwff[:, :, IDX_H:IDX_H + FOX_H],
                                        bf[:, :].unsqueeze(1).broadcast_to((P, NT + 1, FOX_H)), ALU.add))
            settled()
            nc.vector.scalar_tensor_tensor(az[:, :, :], zf[:, :, :], -1.0, zf[:, :, :], ALU.mult, ALU.max)\
                .then_inc(z_done, 1)
            for t, r0, rows in TILES:
                dve.wait_ge(i_hi, t + 1)
                src = pi[:, (t % 6) * 512:(t % 6) * 512 + 3 * P].rearrange("p (a r) -> p a r", a=3)
                nc.vector.tensor_tensor(iT_lo[:, :, r0:r0 + rows], src[:, :, 0:rows],
                                        f32(iT_hi[:, :, r0:r0 + rows]), ALU.subtract).then_inc(i_lo, 1)
            dve.wait_ge(i_lo, NT + 1)
            nc.vector.tensor_tensor(iT_new[:, :, :], f32(iT_hi[:, :, SEQ:ROWS]), f32(iT_lo[:, :, SEQ:ROWS]),
                                    ALU.add).then_inc(i_new, 1)
            dve.wait_ge(l_done, 2)
            nc.vector.scalar_tensor_tensor(c["logf"][:, :, :], zf[:, :, :], 0.0, lz[:, :, :], ALU.min,
                                           ALU.subtract).then_inc(logf_done, 1)
            for i, (j, h) in enumerate(IDX):
                t, at, rows, L = SEG[j]
                dve.wait_ge(i_relu, i + 1)
                w = iwff[0:rows, t, h:h + 1]
                out, r = score[0:rows, at:at + L], relu[i % 2][0:rows, 0:L]
                if h == 0:
                    nc.vector.tensor_scalar(out, r, w, 0.0, ALU.mult, ALU.add).then_inc(i_sum, 1)
                    continue
                dve.wait_ge(i_sum, i)
                nc.vector.scalar_tensor_tensor(out, r, w, out, ALU.mult, ALU.add).then_inc(i_sum, 1)
                if h == IDX_H - 1:
                    dve.wait_ge(i_sum, i + 1)
                    if t < NT:
                        did(nc.vector.memset(score[0:CHUNK, at + L - CHUNK:at + L], LOWEST))
                        settled()
                    key_of(j)

            rel = [0]

            def one(ins):
                rel[0] += 1
                ins.then_inc(step, 1)

            def number(op, plane, j, limit):
                return nc.vector.tensor_scalar(flags(j), plane(j), limit[0:SEG[j][2], j:j + 1], 0.0, op, ALU.add,
                                               accum_out=cnt[0:SEG[j][2], j:j + 1])

            def count(base, plane, j):
                dve.wait_ge(step, base + rel[0] - (0 if j == 0 else 1))
                one(number(ALU.is_ge, plane, j, candidate))

            def next_candidate(base, part, s):
                cols, b = SETS[part], bit[:, part:part + 1]
                dve.wait_ge(step, base + rel[0] - 1)
                if s == 0:
                    one(nc.vector.tensor_tensor(reached[:, cols], cnt[:, cols], want[:, cols], ALU.is_ge))
                elif s == 1:
                    one(nc.vector.scalar_tensor_tensor(low[:, cols], reached[:, cols], b, low[:, cols],
                                                       ALU.mult, ALU.add))
                    one(nc.vector.tensor_scalar(b, b, 0.5, None, ALU.mult))
                else:
                    one(nc.vector.tensor_scalar(candidate[:, cols], low[:, cols], b, None, ALU.add))

            def phase(base, plane, part):
                for i, j in enumerate(range(NSEG)[SETS[part]]):
                    count(base, plane, j)
                    if i < 3:
                        next_candidate(base, 1 - part, i)

            def search(plane, lowest):
                settled()
                did(nc.vector.memset(low[:, :], lowest))
                did(nc.vector.memset(candidate[:, :], lowest + 2.0 ** 15))
                did(nc.vector.memset(bit[:, :], 2.0 ** 15))
                settled()
                for j in range(NSEG)[SETS[0]]:
                    if j >= 2:
                        dve.wait_ge(step, n[0] - 1)
                    did(number(ALU.is_ge, plane, j, candidate))
                per, start = 3 * (NSEG + 8), n[0]
                with dve.Fori(0, 5) as it:
                    rel[0] = 0
                    for part in 3 * (1, 0):
                        phase(it * per + start, plane, part)
                    assert rel[0] == per
                n[0] = start + 5 * per
                rel[0] = 0
                phase(n[0], plane, 1)
                n[0] += rel[0]
                settled()
                cols = SETS[1]
                did(nc.vector.tensor_tensor(reached[:, cols], cnt[:, cols], want[:, cols], ALU.is_ge))
                settled()
                did(nc.vector.tensor_tensor(low[:, cols], reached[:, cols], low[:, cols], ALU.add))
                settled()

            def still_wanted(plane, limit):
                for j in range(NSEG):
                    if j >= 2:
                        dve.wait_ge(step, n[0] - 1)
                    did(number(ALU.is_gt, plane, j, limit))
                settled()
                did(nc.vector.tensor_tensor(want[:, :], want[:, :], cnt[:, :], ALU.subtract))

            dve.wait_ge(planes_done, NSEG)
            search(hi_plane, -2.0 ** 15)
            did(nc.vector.tensor_copy(top_key[:, :], low[:, :]))
            settled()
            still_wanted(hi_plane, top_key)
            for j in range(NSEG):
                did(nc.vector.scalar_tensor_tensor(lo_plane(j), hi_plane(j), top_key[0:SEG[j][2], j:j + 1],
                                                   lo_plane(j), ALU.is_equal, ALU.mult))
            search(lo_plane, 0.0)
            still_wanted(lo_plane, low)
            settled()
            for j0 in range(0, NSEG, 2):
                pair = range(j0, min(NSEG, j0 + 2))
                for s in range(7):
                    for i, j in enumerate(pair):
                        rows = SEG[j][2]
                        e, r = flags(j), ranks(j)
                        top, lo, w = (x[0:rows, j:j + 1] for x in (top_key, low, want))
                        if s == 0:
                            if j >= 2:
                                dve.wait_ge(step, n[0] - i)
                            did(nc.vector.tensor_scalar(e, lo_plane(j), lo, None, ALU.is_equal))
                            continue
                        dve.wait_ge(step, n[0] - (len(pair) - 1))
                        if s == 1:
                            did(nc.vector.scalar_tensor_tensor(e, hi_plane(j), top, e, ALU.is_equal, ALU.mult))
                        elif s == 2:
                            did(nc.vector.tensor_tensor_scan(r, e, e, 0.0, ALU.add, ALU.bypass))
                        elif s == 3:
                            did(nc.vector.scalar_tensor_tensor(e, r, w, e, ALU.is_le, ALU.mult))
                        elif s == 4:
                            did(nc.vector.scalar_tensor_tensor(e, lo_plane(j), lo, e, ALU.is_gt, ALU.add))
                        elif s == 5:
                            did(nc.vector.scalar_tensor_tensor(e, hi_plane(j), top, e, ALU.is_gt, ALU.add))
                        else:
                            _, at, rows, L = SEG[j]
                            did(nc.vector.tensor_scalar(score[0:rows, at:at + L], e, BIG, -BIG, ALU.mult, ALU.add))
            settled()

BH = 4
LAG = 3
BANKS = 4 - LAG


class Item:

    def __init__(self, tile, head, keys, sample=False):
        self.tile, self.head, self.keys, self.sample = tile, head, keys, sample


class Batch:

    def __init__(self, b, items, group):
        self.b, self.items, self.group = b, items, group
        self.sample = items[0].sample
        self.keys = max(it.keys for it in items)
        for i, it in enumerate(items):
            it.batch, it.i = self, i
            it.at = sum(o.keys for o in items[:i])
        blocks = [(k, min(P, self.keys - k)) for k in range(0, self.keys, P)]
        self.steps = [blocks[i:i + 4] for i in range(0, len(blocks), 4)] if self.sample else [[k] for k in blocks]


class Step:

    def __init__(self, kind, batch, part=None):
        self.kind, self.batch, self.part = kind, batch, part


def schedule(batches):
    order, due, copies = [], [], 0

    def give(step):
        order.append(("step", step))

    for it in reversed(batches[0].items):
        order.append(("logits", it))
    for n, batch in enumerate(batches):
        ahead = list(reversed(batches[n + 1].items)) if n + 1 < len(batches) else []
        each = -(-len(ahead) // len(batch.steps))
        for i in range(len(batch.steps)):
            for it in ahead[i * each:(i + 1) * each]:
                order.append(("logits", it))
            give(Step("chunk" if batch.sample else "block", batch, i))
            copies += 1
            while due and copies >= due[0][0]:
                give(due.pop(0)[1])
        due.append((copies + LAG + 1, Step("finish" if batch.sample else "out", batch)))
    for _, step in due:
        give(step)
    n = m = copy = split = 0
    for what, x in order:
        if what == "logits":
            x.n, n = n, n + 1
            continue
        x.m, x.copy, x.split = m, copy, split
        m += x.kind != "finish"
        copy += x.kind in ("block", "chunk")
        split += x.kind == "block"
        if x.kind in ("block", "chunk"):
            x.batch.last = x
            if x.part == 0:
                x.batch.first = x
    return order


def attention(nc, ctx, pl, areas, c, tag, batches, v, v_loaded, loads, pe_first, act_first, dve_first, logits, bias,
              sample_values, sample_cols, out_view, out_sample):
    def sem(name):
        return ctx.enter_context(nc.semaphore(f"{tag}_{name}"))

    ident = c["ident"]
    order = schedule(batches)
    steps = [x for what, x in order if what == "step"]
    banked = [x for x in steps if x.kind != "finish"]
    copied = [x for x in steps if x.kind in ("block", "chunk")]
    N = sum(len(b.items) for b in batches)
    groups = sorted({b.group for b in batches if not b.sample})
    opens = {min(b.b for b in batches if b.group == g): g for g in groups}
    closes = {g: max(b.b for b in batches if b.group == g) for g in groups}

    big = areas(f"{tag}_exp_even", [P, max(sum(it.keys for it in b.items) for b in batches[0::2])], F32)
    small = areas(f"{tag}_exp_odd", [P, max(sum(it.keys for it in b.items) for b in batches[1::2])], F32)
    v_parts = [pl(f"{tag}_v_parts{s}", [P, NT, 2 * HD], F32R) for s in range(2)]
    whole = Places(nc, pl.at, c["end"])
    eT = [whole(f"{tag}_eT{s}", [P, 4 * P], F32) for s in range(LAG)]
    eT_hi = [pl(f"{tag}_eT_hi{s}", [P, 4 * P], F32R) for s in range(LAG)]
    eT_lo = [pl(f"{tag}_eT_lo{s}", [P, 4 * P], F32R) for s in range(LAG)]
    oT = pl(f"{tag}_oT", [P, 4 * P], F32)
    nmax = pl(f"{tag}_nmax", [P, 4], F32)
    rsum = pl(f"{tag}_rsum", [P, 4, BH], F32)
    rinv = pl(f"{tag}_rinv", [P, BH], F32)
    ps = ctx.enter_context(nc.psum_tensor(f"{tag}_logits", [P, 4 * 512], F32))
    pt = ctx.enter_context(nc.psum_tensor(f"{tag}_transposed", [P, LAG, 512], F32))
    po = ctx.enter_context(nc.psum_tensor(f"{tag}_outputs", [P, BANKS, 512], F32))
    c["ps"] = ps
    qk_done, biased_done, exp_done = sem("qk_done"), sem("biased_done"), sem("exp_done")
    tr_done, hi_done, lo_done, pv_done = sem("tr_done"), sem("hi_done"), sem("lo_done"), sem("pv_done")
    o_copied, out_done, dve_step = sem("o_copied"), sem("out_done"), sem("dve_step")
    v_hi_done, v_lo_done = sem("v_hi_done"), sem("v_lo_done")
    c["sems"] = {"biased_done": biased_done, "out_done": out_done, "v_lo_done": v_lo_done}
    block = ctx.enter_context(nc.Block())

    def exps(it):
        area = big if it.batch.b % 2 == 0 else small
        return area[:, it.at:it.at + it.keys]

    def logits_at(it):
        at = 0 if it.sample else 1024 * (it.n % 2)
        return ps[:, at:at + it.keys]

    def out_number(batch):
        return 1 + sum(x.kind in ("out", "finish") for x in steps[:steps.index(
            next(x for x in steps if x.kind in ("out", "finish") and x.batch is batch))])

    @block.sync
    def _(sp):
        loads(sp)
        sp.wait_ge(out_done, len(batches))

    @block.tensor
    def _(pe):
        pe_first(pe)

        def transposes(x):
            if x.kind == "out":
                pe.wait_ge(o_copied, x.batch.b + 1)
            elif x.part == 0:
                pe.wait_ge(exp_done, max(it.n for it in x.batch.items) + 1)
            if x.m >= LAG:
                y = banked[x.m - LAG]
                if y.kind == "out":
                    pe.wait_ge(out_done, out_number(y.batch))
                elif y.kind == "block":
                    pe.wait_ge(lo_done, y.split + 1)
                else:
                    pe.wait_ge(hi_done, y.copy + 1)
            if x.kind == "out":
                for i in range(BH):
                    mm = nc.tensor.transpose(pt[:, x.m % LAG, i * P:(i + 1) * P], oT[:, i * P:(i + 1) * P], ident[:, :])
            elif x.kind == "chunk":
                e = exps(x.batch.items[0])
                for i, (k0, kn) in enumerate(x.batch.steps[x.part]):
                    mm = nc.tensor.transpose(pt[0:kn, x.m % LAG, i * P:(i + 1) * P], e[:, k0:k0 + kn], ident[:, :])
            else:
                k0 = x.batch.steps[x.part][0][0]
                for it in x.batch.items:
                    if k0 < it.keys:
                        mm = nc.tensor.transpose(pt[:, x.m % LAG, it.i * P:(it.i + 1) * P], exps(it)[:, k0:k0 + P],
                                                 ident[:, :])
            mm.then_inc(tr_done, 1)

        def weighted(x):
            batch, s, o = x.batch, x.copy % LAG, x.batch.b % BANKS
            if x is batch.first and batch.b >= BANKS:
                if batches[batch.b - BANKS].sample:
                    pe.wait_ge(out_done, out_number(batches[batch.b - BANKS]))
                else:
                    pe.wait_ge(o_copied, batch.b - BANKS + 1)
            last = x is batch.last
            if x.kind == "chunk":
                pe.wait_ge(hi_done, x.copy + 1)
                for i, (k0, kn) in enumerate(batch.steps[x.part]):
                    mm = nc.tensor.matmul(po[:, o, 0:sample_cols], eT[s][0:kn, i * P:(i + 1) * P],
                                          sample_values(pe, batch.items[0], k0, kn), start=(x.part == 0 and i == 0),
                                          stop=(last and i == len(batch.steps[x.part]) - 1))
            else:
                if x is batch.first and batch.b in opens:
                    pe.wait_ge(v_lo_done, groups.index(batch.group) + 1)
                pe.wait_ge(lo_done, x.split + 1)
                i0 = min(it.i for it in batch.items if batch.steps[x.part][0][0] < it.keys)
                vp, cols = v_parts[batch.group % 2], slice(i0 * P, BH * P)
                nc.tensor.matmul(po[:, o, cols], vp[:, x.part, :], eT_hi[s][:, cols], start=x is batch.first,
                                 stop=False, skip_group_check=True)
                mm = nc.tensor.matmul(po[0:HD, o, cols], vp[:, x.part, 0:HD], eT_lo[s][:, cols], start=False,
                                      stop=last, skip_group_check=True)
            mm.then_inc(pv_done, 1)

        done = 0
        for what, x in order:
            if what == "logits":
                if x.sample and x.n >= 1:
                    pe.wait_ge(biased_done, x.n)
                elif x.n >= 2:
                    pe.wait_ge(biased_done, x.n - 1)
                logits(pe, x, logits_at(x)).then_inc(qk_done, 1)
                continue
            if x.kind != "finish":
                transposes(x)
            upto = x.copy - LAG + 1 if x.kind in ("block", "chunk") else x.batch.last.copy + 1
            while done < upto:
                weighted(copied[done])
                done += 1
            if x is copied[-1]:
                while done < len(copied):
                    weighted(copied[done])
                    done += 1

    @block.scalar
    def _(act):
        act_first(act)
        waiting, gone = [], []

        def exp(it):
            b = it.batch.b
            act.wait_ge(biased_done, it.n + 1)
            if b >= 4:
                act.wait_ge(out_done, out_number(batches[b - 4]))
            nc.scalar.activation(exps(it), exps(it), ACT.Exp, scale=-1.0, bias=nmax[:, it.n % 4:it.n % 4 + 1],
                                 accum_out=rsum[:, b % 4, it.i:it.i + 1]).then_inc(exp_done, 1)

        def hi(x):
            act.wait_ge(tr_done, x.m + 1)
            if x.copy >= LAG:
                act.wait_ge(pv_done, x.copy - LAG + 1)
            blocks, s, bank = x.batch.steps[x.part], x.copy % LAG, pt[:, x.m % LAG, :]
            if x.kind == "chunk":
                full, rest = sum(kn == P for _, kn in blocks) * P, blocks[-1][1]
                if full:
                    last = nc.scalar.copy(eT[s][:, 0:full], bank[:, 0:full])
                if rest < P:
                    last = nc.scalar.copy(eT[s][0:rest, full:full + P], bank[0:rest, full:full + P])
            else:
                i0 = min(it.i for it in x.batch.items if blocks[0][0] < it.keys)
                last = nc.scalar.copy(eT_hi[s][:, i0 * P:], bank[:, i0 * P:])
            last.then_inc(hi_done, 1)

        for what, x in order:
            if what == "logits":
                b = x.batch
                if b.b in opens and x is b.items[-1]:
                    if b.group == groups[0]:
                        act.wait_ge(v_loaded, 16)
                    if groups.index(b.group) >= 2:
                        act.wait_ge(pv_done, batches[closes[b.group - 2]].last.copy + 1)
                    nc.scalar.copy(v_parts[b.group % 2][:, :, 0:HD], v[:, :, b.group * HD:(b.group + 1) * HD])\
                        .then_inc(v_hi_done, 1)
                waiting.append(x)
                continue
            for y in (x, *steps[steps.index(x) + 1:steps.index(x) + 2]):
                if y.kind == "out" and y not in gone:
                    act.wait_ge(pv_done, y.batch.last.copy + 1)
                    if gone:
                        act.wait_ge(tr_done, gone[-1].m + 1)
                    nc.scalar.copy(oT[:, :], po[:, y.batch.b % BANKS, :]).then_inc(o_copied, 1)
                    gone.append(y)
            if x.kind in ("block", "chunk"):
                for it in [it for it in waiting if it.batch is x.batch]:
                    exp(it)
                    waiting.remove(it)
                hi(x)
            for it in waiting:
                exp(it)
            waiting = []

    @block.vector
    def _(dve):
        dve_first(dve)
        n = [0]

        def settled(ins):
            n[0] += 1
            ins.then_inc(dve_step, 1)
            dve.wait_ge(dve_step, n[0])

        def biased_max(it):
            in1, b = bias(dve, it), it.batch.b
            if b >= 2:
                dve.wait_ge(tr_done, batches[b - 2].last.m + 1)
            dve.wait_ge(qk_done, it.n + 1)
            if it.n >= 4:
                dve.wait_ge(exp_done, it.n - 3)
            one = slice(it.n % 4, it.n % 4 + 1)
            nc.vector.tensor_tensor_reduce(exps(it), logits_at(it), in1, -1.0, 3.3e38, ALU.add, ALU.min,
                                           nmax[:, one]).then_inc(biased_done, 1)

        for what, x in order:
            if what == "logits":
                b = x.batch
                if b.b in opens and x is b.items[-1]:
                    g = b.group
                    dve.wait_ge(v_hi_done, groups.index(g) + 1)
                    nc.vector.tensor_tensor(v_parts[g % 2][:, :, HD:2 * HD], v[:, :, g * HD:(g + 1) * HD],
                                            f32(v_parts[g % 2][:, :, 0:HD]), ALU.subtract).then_inc(v_lo_done, 1)
                biased_max(x)
            elif x.kind == "block":
                dve.wait_ge(hi_done, x.copy + 1)
                i0, s = min(it.i for it in x.batch.items if x.batch.steps[x.part][0][0] < it.keys), x.copy % LAG
                nc.vector.tensor_tensor(eT_lo[s][:, i0 * P:], pt[:, x.m % LAG, i0 * P:], f32(eT_hi[s][:, i0 * P:]),
                                        ALU.subtract).then_inc(lo_done, 1)
            elif x.kind == "out":
                dve.wait_ge(exp_done, max(it.n for it in x.batch.items) + 1)
                if out_number(x.batch) >= 2:
                    dve.wait_ge(out_done, out_number(x.batch) - 1)
                settled(nc.vector.reciprocal(rinv[:, :], rsum[:, x.batch.b % 4, :]))
                dve.wait_ge(tr_done, x.m + 1)
                parts = pt[:, x.m % LAG, :].rearrange("p (i e) -> p i e", e=P)
                out = out_view(x.batch)
                settled(nc.vector.tensor_copy(out, parts[:, :, 0:HD]))
                settled(nc.vector.tensor_tensor(out, out, parts[:, :, HD:2 * HD], ALU.add))
                nc.vector.tensor_tensor(out, out, rinv[:, :].unsqueeze(2).broadcast_to((P, BH, HD)), ALU.mult)\
                    .then_inc(out_done, 1)
            elif x.kind == "finish":
                dve.wait_ge(exp_done, x.batch.items[0].n + 1)
                dve.wait_ge(out_done, out_number(x.batch) - 1)
                settled(nc.vector.reciprocal(rinv[:, 0:1], rsum[:, x.batch.b % 4, 0:1]))
                dve.wait_ge(pv_done, x.batch.last.copy + 1)
                for j in range(4):
                    rows, c0 = slice(j * NEW, (j + 1) * NEW), j * HD if sample_cols > HD else 0
                    last = nc.vector.tensor_scalar(out_sample(x.batch.items[0], j), po[rows, x.batch.b % BANKS, c0:c0 + HD],
                                                   rinv[rows, 0:1], None, ALU.mult)
                last.then_inc(out_done, 1)



def fox(nc, d, c):
    from contextlib import ExitStack
    with ExitStack() as ctx:
        def sem(name):
            return ctx.enter_context(nc.semaphore(name))

        pl = Places(nc, c["after_mix"], c["end"])
        v = pl("fox_v", [P, NT, 512], F32)
        v_new = pl("fox_v_new", [NEW, 512], F32)
        kT_past = pl("fox_kT_past", [P, 2, PAST], F32)
        kT_new = pl("fox_kT_new", [P, 4, NEW], F32)
        q_diag = pl("q_diag", [P, 4, P], F32)
        key_bias = [pl(f"key_bias{s}", [P, SEQ], F32) for s in range(2)]
        key_bias_s = pl("key_bias_s", [P, KEYS_S], F32)
        kT_hi, kT_lo, qT_hi, qT_lo = c["kT_hi"], c["kT_lo"], c["qT_hi"], c["qT_lo"]
        mix, logf, ident = c["mix"], c["logf"], c["ident"]
        m0 = Places(nc, c["rest"], c["after_mix"])
        ones = m0("ones", [FOX_H, SEQ], F32)
        negc = m0("negc", [FOX_H, SEQ], F32)
        bias_s = m0("bias_s", [FOX_H, KEYS_S], F32)
        lf_past = m0("lf_past", [FOX_H, PAST], F32)

        batches = [Batch(2 * h + half, [Item(t, h, (t + 1) * P) for t in range(4 - 4 * half, 8 - 4 * half)], h)
                   for h in range(FOX_H) for half in range(2)]
        batches += [Batch(2 * FOX_H + q, [Item(NT, 4 * q, KEYS_S, True)], None) for q in range(2)]
        lf_loaded, v_loaded, vs_loaded = sem("lf_loaded"), sem("v_loaded"), sem("vs_loaded")
        kp_loaded, bias_stored = sem("kp_loaded"), sem("bias_stored")
        kb_loaded = [sem(f"kb_loaded{s}") for s in range(2)]
        kbs_loaded, kbs_ready = sem("kbs_loaded"), sem("kbs_ready")
        lfT_done, c_done, start_step, diag_done = sem("lfT_done"), sem("c_done"), sem("start_step"), sem("diag_done")
        S = c

        def loads(sp):
            s = S["sems"]
            sp.dma_start(lf_past[:, :], d["past_logfT"]).then_inc(lf_loaded, 16)
            sp.dma_start(v[:, :, :], d["fv"][0:SEQ, :].rearrange("(t p) n -> p t n", p=P)).then_inc(v_loaded, 16)
            sp.wait_ge(c_done, 3)
            sp.dma_start(d["negc"], negc[:, :]).then_inc(bias_stored, 16)
            sp.dma_start(d["bias_s"], bias_s[:, :]).then_inc(bias_stored, 16)
            sp.wait_ge(bias_stored, 32)
            for h in range(FOX_H):
                if h >= 2:
                    sp.wait_ge(s["biased_done"], 8 * (h - 1))
                sp.dma_start(key_bias[h % 2][:, :], d["negc"][h].partition_broadcast(P)).then_inc(kb_loaded[h % 2], 16)
                if h == 1:
                    sp.dma_start(v_new[:, :], d["fv"][SEQ:ROWS, :]).then_inc(vs_loaded, 16)
            sp.wait_ge(s["v_lo_done"], FOX_H)
            sp.dma_start(v[:, :, :], d["past_fv"].rearrange("(t p) n -> p t n", p=P)).then_inc(vs_loaded, 16)
            for q in range(2):
                if q:
                    sp.wait_ge(s["biased_done"], 65)
                sp.dma_start(kT_past[:, :, :], d["past_fkT"][q * 256:(q + 1) * 256, :].rearrange(
                    "(a p) n -> p a n", p=P)).then_inc(kp_loaded, 16)
                for j in range(4):
                    sp.dma_start(key_bias_s[j * NEW:(j + 1) * NEW, :], d["bias_s"][4 * q + j].partition_broadcast(NEW))\
                        .then_inc(kbs_loaded, 16)

        def pe_first(pe):
            ps = S["ps"]
            for t, r0, rows in TILES:
                at = r0 if t < NT else SEQ
                mm = nc.tensor.transpose(ps[0:FOX_H, at:at + rows], logf[0:rows, t, :], ident[0:rows, 0:rows])
            mm.then_inc(lfT_done, 1)
            pe.wait_ge(c_done, 4)
            pe.wait_ge(diag_done, 1)

        def dve_first(dve):
            ps = S["ps"]
            nc.vector.memset(ones[:, :], 1.0).then_inc(start_step, 1)
            nc.vector.memset(q_diag[:, :, :], 0.0).then_inc(start_step, 1)
            nc.vector.memset(bias_s[:, PAST - 1:PAST], 0.0).then_inc(start_step, 1)
            dve.wait_ge(start_step, 3)
            dve.wait_ge(lf_loaded, 16)
            nc.vector.tensor_tensor_scan(bias_s[:, 0:PAST - 1][:, ::-1], ones[:, 0:PAST - 1], lf_past[:, 1:PAST][:, ::-1],
                                         0.0, ALU.mult, ALU.add).then_inc(c_done, 1)
            dve.wait_ge(lfT_done, 1)
            nc.vector.tensor_tensor_scan(negc[:, :], ones[:, :], ps[0:FOX_H, 0:SEQ], 0.0, ALU.mult, ALU.subtract)\
                .then_inc(c_done, 1)
            nc.vector.tensor_tensor_scan(bias_s[:, PAST:KEYS_S], ones[:, 0:NEW], ps[0:FOX_H, SEQ:ROWS], 0.0, ALU.mult,
                                         ALU.subtract).then_inc(c_done, 1)
            nc.vector.tensor_tensor(kT_new[:, :, :], f32(kT_hi[:, :, SEQ:ROWS]), f32(kT_lo[:, :, SEQ:ROWS]), ALU.add)\
                .then_inc(c_done, 1)
            for a in range(4):
                for r in range(2):
                    part = slice(r * HD, (r + 1) * HD)
                    col = ((2 * a + r) % 4) * NEW
                    last = nc.vector.tensor_tensor(q_diag[part, a, col:col + NEW], f32(qT_hi[part, a, SEQ:ROWS]),
                                                   f32(qT_lo[part, a, SEQ:ROWS]), ALU.add)
            last.then_inc(diag_done, 1)

        def bias(dve, it):
            if not it.sample:
                dve.wait_ge(kb_loaded[it.head % 2], 16 * (it.head // 2 + 1))
                return key_bias[it.head % 2][:, 0:it.keys]
            q = it.head // 4
            dve.wait_ge(kbs_loaded, 64 * (q + 1))
            return key_bias_s[:, :]

        def logits(pe, it, out):
            if not it.sample:
                part, a = slice(HD * (it.head % 2), HD * (it.head % 2) + HD), it.head // 2
                qs = slice(it.tile * P, (it.tile + 1) * P)
                for k0 in range(0, it.keys, 512):
                    ks = slice(k0, min(it.keys, k0 + 512))
                    o = out[:, ks]
                    nc.tensor.matmul(o, qT_hi[part, a, qs], kT_hi[part, a, ks], start=True, stop=False)
                    nc.tensor.matmul(o, qT_hi[part, a, qs], kT_lo[part, a, ks], start=False, stop=False)
                    mm = nc.tensor.matmul(o, qT_lo[part, a, qs], kT_hi[part, a, ks], start=False, stop=ks.stop < it.keys)
                return nc.tensor.matmul(out[:, it.keys - P:it.keys], c["ident16"][:, :], c["causal16"][:, :],
                                        start=False, stop=True)
            q = it.head // 4
            pe.wait_ge(kp_loaded, 16 * (q + 1))
            for k0 in range(0, PAST, 512):
                for a in range(2):
                    nc.tensor.matmul(out[:, k0:k0 + 512], q_diag[:, 2 * q + a, :], kT_past[:, a, k0:k0 + 512],
                                     start=a == 0, stop=a == 1)
            for a in range(2):
                nc.tensor.matmul(out[:, PAST:KEYS_S], q_diag[:, 2 * q + a, :], kT_new[:, 2 * q + a, :],
                                 start=a == 0, stop=False)
            return nc.tensor.matmul(out[:, PAST:KEYS_S], c["ident16"][:, :], c["causal_s16"][:, :], start=False, stop=True)

        def sample_values(pe, it, k0, kn):
            cols = slice(it.head * HD, (it.head + 4) * HD)
            if it.head == 0 and k0 == 0:
                pe.wait_ge(vs_loaded, 32)
            return v[:, k0 // P, cols] if k0 < PAST else v_new[0:kn, cols]

        def out_view(batch):
            it = batch.items[0]
            return mix[:, it.tile:it.tile + BH, it.head * HD:(it.head + 1) * HD]

        def out_sample(it, j):
            return mix[0:NEW, NT, (it.head + j) * HD:(it.head + j + 1) * HD]

        attention(nc, ctx, pl, pl, c, "fox", batches, v, v_loaded, loads, pe_first, lambda act: None, dve_first,
                  logits, bias, sample_values, 4 * HD, out_view, out_sample)



def dsa(nc, d, c):
    from contextlib import ExitStack
    with ExitStack() as ctx:
        def sem(name):
            return ctx.enter_context(nc.semaphore(name))

        pl = Places(nc, c["after_mix"], c["end"])
        start = pl.at
        q_row = pl("dsa_q_row", [P, NT + 1, 512], F32)
        k_row = pl("dsa_k_row", [P, NT + 1, KV_H, 2, HD], F32)
        areas = Places(nc, start, pl.at)
        v = pl("dsa_v", [P, NT, P], F32)
        v_past = pl("dsa_v_past", [P, NT, P], F32)
        v_new = pl("dsa_v_new", [NEW, P], F32)
        kT_past = pl("dsa_kT_past", [P, 2, PAST], F32)
        kT_new = pl("dsa_kT_new", [P, 2, NEW], F32)
        q_diag = pl("dsa_q_diag", [P, 4, P], F32)
        mask_s = pl("mask_s", [P, KEYS_S], F32)
        kT_hi, kT_lo, qT_hi, qT_lo = c["kT_hi"], c["kT_lo"], c["qT_hi"], c["qT_lo"]
        mix, ident, score, corner = c["mix"], c["ident"], c["score"], c["corner"]

        half = NT // 2
        falling = [t for i in range(half) for t in (NT - 1 - i, half - 1 - i)]
        rising = [t for i in range(half) for t in (half + i, (i + 1) % half)]
        batches = [Batch(NT * g + i, [Item(t, 4 * g + j, (t + 1) * P) for j in range(BH)], g)
                   for g, tiles in enumerate((falling, rising)) for i, t in enumerate(tiles)]
        batches += [Batch(NT * KV_H + q, [Item(NT, 4 * q, KEYS_S, True)], None) for q in range(2)]
        q_loaded = [sem(f"q_loaded{t}") for t in range(NT + 1)]
        k_loaded, v_loaded, vs_loaded = sem("k_loaded"), sem("v_loaded"), sem("vs_loaded")
        kp_loaded, mask_loaded = sem("kp_loaded"), sem("mask_loaded")
        k_twice = sem("k_twice")
        h_tr, h_hi, h_lo, diag_done, zeroed = sem("h_tr"), sem("h_hi"), sem("h_lo"), sem("diag_done"), sem("zeroed")
        S = c

        def loads(sp):
            for g in range(KV_H):
                cols = slice(g * HD, (g + 1) * HD)
                sp.dma_start(k_row[:, 0:NT, g, 0, :], d["dk"][0:SEQ, cols].rearrange("(t p) n -> p t n", p=P))\
                    .then_inc(k_loaded, 16)
                sp.dma_start(k_row[0:NEW, NT, g, 0, :], d["dk"][SEQ:ROWS, cols]).then_inc(k_loaded, 16)
            for t, r0, rows in TILES:
                sp.dma_start(q_row[0:rows, t, :], d["dq"][r0:r0 + rows, :]).then_inc(q_loaded[t], 16)
            sp.dma_start(v[:, :, :], d["dv"][0:SEQ, :].rearrange("(t p) n -> p t n", p=P)).then_inc(v_loaded, 16)
            sp.dma_start(v_past[:, :, :], d["past_dv"].rearrange("(t p) n -> p t n", p=P)).then_inc(vs_loaded, 16)
            sp.dma_start(v_new[:, :], d["dv"][SEQ:ROWS, :]).then_inc(vs_loaded, 16)
            for r in range(2):
                for g in range(KV_H):
                    sp.dma_start(kT_past[r * HD:(r + 1) * HD, g, :], d["past_dkT"][g * HD:(g + 1) * HD, :])\
                        .then_inc(kp_loaded, 16)
            at = SEG[-1][1]
            for j in range(4):
                sp.dma_start(mask_s[j * NEW:(j + 1) * NEW, :], score[0:NEW, at:at + KEYS_S]).then_inc(mask_loaded, 16)

        def pe_first(pe):
            ps = S["ps"]
            pe.wait_ge(k_twice, 2)
            for t, r0, rows in TILES:
                pe.wait_ge(q_loaded[t], 16)
                if t >= 2:
                    pe.wait_ge(h_lo, t - 1)
                o = 1024 * (t % 2)
                for a in range(4):
                    nc.tensor.transpose(ps[:, o + a * P:o + a * P + rows], q_row[0:rows, t, a * P:(a + 1) * P],
                                        ident[0:rows, 0:rows])
                for g in range(KV_H):
                    mm = nc.tensor.transpose(ps[:, o + 512 + g * P:o + 512 + g * P + rows],
                                             k_row[0:rows, t, g, :, :].rearrange("p r e -> p (r e)"),
                                             ident[0:rows, 0:rows])
                mm.then_inc(h_tr, 1)
            pe.wait_ge(h_lo, NT + 1)
            pe.wait_ge(diag_done, 2)

        def views(t, r0, rows):
            o = 1024 * (t % 2)
            q = S["ps"][:, o:o + 512].rearrange("p (a r) -> p a r", r=P)[:, :, 0:rows]
            k = S["ps"][:, o + 512:o + 768].rearrange("p (a r) -> p a r", r=P)[:, :, 0:rows]
            return q, k, slice(r0, r0 + rows)

        def act_first(act):
            for t, r0, rows in TILES:
                q, k, cols = views(t, r0, rows)
                act.wait_ge(h_tr, t + 1)
                nc.scalar.activation(qT_hi[:, :, cols], q, ACT.Copy, scale=SCALE)
                nc.scalar.copy(kT_hi[:, 0:2, cols], k).then_inc(h_hi, 1)

        def dve_first(dve):
            nc.vector.memset(q_diag[:, :, :], 0.0).then_inc(zeroed, 1)
            dve.wait_ge(k_loaded, 64)
            nc.vector.tensor_copy(k_row[:, 0:NT, :, 1, :], k_row[:, 0:NT, :, 0, :]).then_inc(k_twice, 1)
            nc.vector.tensor_copy(k_row[0:NEW, NT, :, 1, :], k_row[0:NEW, NT, :, 0, :]).then_inc(k_twice, 1)
            for t, r0, rows in TILES:
                q, k, cols = views(t, r0, rows)
                dve.wait_ge(h_hi, t + 1)
                nc.vector.scalar_tensor_tensor(qT_lo[:, :, cols], q, SCALE, f32(qT_hi[:, :, cols]), ALU.mult,
                                               ALU.subtract)
                nc.vector.tensor_tensor(kT_lo[:, 0:2, cols], k, f32(kT_hi[:, 0:2, cols]), ALU.subtract)\
                    .then_inc(h_lo, 1)
            dve.wait_ge(h_lo, NT + 1)
            dve.wait_ge(zeroed, 1)
            nc.vector.tensor_tensor(kT_new[:, :, :], f32(kT_hi[:, 0:2, SEQ:ROWS]), f32(kT_lo[:, 0:2, SEQ:ROWS]), ALU.add)\
                .then_inc(diag_done, 1)
            for a in range(4):
                for r in range(2):
                    part = slice(r * HD, (r + 1) * HD)
                    col = ((2 * a + r) % 4) * NEW
                    last = nc.vector.tensor_tensor(q_diag[part, a, col:col + NEW], f32(qT_hi[part, a, SEQ:ROWS]),
                                                   f32(qT_lo[part, a, SEQ:ROWS]), ALU.add)
            last.then_inc(diag_done, 1)

        def bias(dve, it):
            if it.sample:
                dve.wait_ge(mask_loaded, 64)
                return mask_s[:, :]
            if it.keys <= TOPK:
                return corner[:, 2 * P - it.keys:2 * P]
            at = SEG[it.tile - TOPK // P][1]
            return score[:, at:at + it.keys]

        def logits(pe, it, out):
            g = it.head // 4
            if not it.sample:
                part, a = slice(HD * (it.head % 2), HD * (it.head % 2) + HD), it.head // 2
                qs = slice(it.tile * P, (it.tile + 1) * P)
                for k0 in range(0, it.keys, 512):
                    ks = slice(k0, min(it.keys, k0 + 512))
                    o = out[:, ks]
                    nc.tensor.matmul(o, qT_hi[part, a, qs], kT_hi[part, g, ks], start=True, stop=False)
                    nc.tensor.matmul(o, qT_hi[part, a, qs], kT_lo[part, g, ks], start=False, stop=False)
                    mm = nc.tensor.matmul(o, qT_lo[part, a, qs], kT_hi[part, g, ks], start=False, stop=True)
                return mm
            if g == 0:
                pe.wait_ge(kp_loaded, 64)
            for k0 in list(range(0, PAST, 512)) + [PAST]:
                k1 = min(k0 + 512, KEYS_S)
                for a in range(2):
                    r = kT_past[:, g, k0:k1] if k0 < PAST else kT_new[:, g, :]
                    mm = nc.tensor.matmul(out[:, k0:k1], q_diag[:, 2 * g + a, :], r, start=a == 0, stop=a == 1)
            return mm

        def sample_values(pe, it, k0, kn):
            g = it.head // 4
            cols = slice(g * HD, (g + 1) * HD)
            if g == 0 and k0 == 0:
                pe.wait_ge(vs_loaded, 32)
            return v_past[:, k0 // P, cols] if k0 < PAST else v_new[0:kn, cols]

        def out_view(batch):
            c0 = 512 + batch.items[0].head * HD
            return mix[:, batch.items[0].tile, c0:c0 + BH * HD].rearrange("p (i e) -> p i e", e=HD)

        def out_sample(it, j):
            c0 = 512 + (it.head + j) * HD
            return mix[0:NEW, NT, c0:c0 + HD]

        attention(nc, ctx, pl, areas, c, "dsa", batches, v, v_loaded, loads, pe_first, act_first, dve_first,
                  logits, bias, sample_values, HD, out_view, out_sample)



class Norm:

    def __init__(self, nc, pl, sem, tag, gain, shift, loaded):
        self.nc, self.gain, self.shift, self.loaded = nc, gain, shift, loaded
        self.stats = pl(tag + "_stats", [P, NT + 1, 12], F32)
        self.mv = pl(tag + "_mv", [P, NT + 1, 2], F32)
        self.ve = pl(tag + "_var_eps", [P, NT + 1], F32)
        self.rstd = pl(tag + "_rstd", [P, NT + 1], F32)
        self.power = pl(tag + "_power", [P, 1], F32)
        self.step, self.var_done, self.rstd_done = sem("ln_step"), sem("ln_var_done"), sem("ln_rstd_done")
        self.n = 0

    def settled(self, dve, ins):
        self.n += 1
        ins.then_inc(self.step, 1)
        dve.wait_ge(self.step, self.n)

    def moments(self, dve, t, rows, y):
        v = self.nc.vector
        v.bn_stats(self.stats[0:rows, t, 0:6], y[:, 0:512])
        self.settled(dve, v.bn_stats(self.stats[0:rows, t, 6:12], y[:, 512:D]))
        self.settled(dve, v.bn_aggr(self.mv[0:rows, t, :], self.stats[0:rows, t, :]))
        v.tensor_scalar(self.ve[0:rows, t:t + 1], self.mv[0:rows, t, 1:2], LN_EPS, None, ALU.add)\
            .then_inc(self.var_done, 1)

    def power_first(self):
        self.nc.gpsimd.memset(self.power[:, :], -0.5).then_inc(self.rstd_done, 1)

    def root(self, pool, t, rows):
        pool.wait_ge(self.rstd_done, 1)
        pool.wait_ge(self.var_done, t + 1)
        self.nc.gpsimd.tensor_tensor(self.rstd[0:rows, t:t + 1], self.ve[0:rows, t:t + 1], self.power[0:rows, :],
                                     ALU.pow).then_inc(self.rstd_done, 1)

    def scaled(self, dve, t, rows, y):
        dve.wait_ge(self.rstd_done, t + 2)
        dve.wait_ge(self.loaded, 32)
        v = self.nc.vector
        self.settled(dve, v.tensor_scalar(y, y, self.mv[0:rows, t, 0:1], self.rstd[0:rows, t:t + 1], ALU.subtract,
                                          ALU.mult))
        return v.tensor_tensor(y, y, self.gain[0:rows, :], ALU.mult)



def mix_out(nc, d, c):
    from contextlib import ExitStack
    with ExitStack() as ctx:
        def sem(name):
            return ctx.enter_context(nc.semaphore(name))

        tp = Places(nc, c["t_region"], c["rest"])
        w_hi = tp("wo_hi", [P, KD, D], F32R)
        w_lo = tp("wo_lo", [P, KD, D], F32R)
        pl = Places(nc, c["after_mix"], c["end"])
        w_raw = [pl(f"wo_raw{s}", [P, D], F32) for s in range(4)]
        mT_hi = [pl(f"mT_hi{s}", [P, KD, P], F32R) for s in range(2)]
        mT_lo = [pl(f"mT_lo{s}", [P, KD, P], F32R) for s in range(2)]
        x_row = [pl(f"x_row{s}", [P, D], F32) for s in range(2)]
        pre = [pl(f"pre{s}", [P, D], F32) for s in range(2)]
        gain, shift = pl("ln1_gain", [P, D], F32), pl("ln1_shift", [P, D], F32)
        mix, ident = c["mix"], c["ident"]
        pt = ctx.enter_context(nc.psum_tensor("mix_T", [P, 4 * 512], F32))
        py = ctx.enter_context(nc.psum_tensor("mixed", [P, 4 * 512], F32))
        w_loaded = [sem(f"wo_loaded{s}") for s in range(4)]
        x_loaded = [sem(f"x_row_loaded{s}") for s in range(2)]
        w_hi_done, w_lo_done, ln_loaded = sem("w_hi_done"), sem("w_lo_done"), sem("ln_loaded")
        tr_done, m_hi, m_lo = sem("mix_transposed"), sem("m_hi"), sem("m_lo")
        product, pre_done, h_done = sem("product"), sem("pre_done"), sem("h_done")
        norm = Norm(nc, pl, sem, "ln1", gain, shift, ln_loaded)
        block = ctx.enter_context(nc.Block())

        @block.sync
        def _(sp):
            def load_x(t):
                _, r0, rows = TILES[t]
                if t >= 2:
                    sp.wait_ge(pre_done, t - 1)
                sp.dma_start(x_row[t % 2][0:rows, :], d["x"][r0:r0 + rows, :]).then_inc(x_loaded[t % 2], 16)

            for k in range(KD):
                if k >= 4:
                    sp.wait_ge(w_lo_done, k - 3)
                sp.dma_start(w_raw[k % 4][:, :], d["w_out"][k * P:(k + 1) * P, :]).then_inc(w_loaded[k % 4], 16)
            load_x(0)
            load_x(1)
            sp.dma_start(gain[:, :], d["ln1_g"].partition_broadcast(P)).then_inc(ln_loaded, 16)
            sp.dma_start(shift[:, :], d["ln1_b"].partition_broadcast(P)).then_inc(ln_loaded, 16)
            for t in range(2, NT + 1):
                load_x(t)
            sp.wait_ge(h_done, NT + 1)

        @block.tensor
        def _(pe):
            def transposes(t):
                _, r0, rows = TILES[t]
                if t >= 2:
                    pe.wait_ge(m_lo, t - 1)
                for k in range(KD):
                    o = 1024 * (t % 2) + k * P
                    mm = nc.tensor.transpose(pt[:, o:o + rows], mix[0:rows, t, k * P:(k + 1) * P],
                                             ident[0:rows, 0:rows])
                mm.then_inc(tr_done, 1)

            transposes(0)
            for t, r0, rows in TILES:
                if t < NT:
                    transposes(t + 1)
                pe.wait_ge(m_lo, t + 1)
                if t >= 2:
                    pe.wait_ge(pre_done, t - 1)
                for half in range(2):
                    cols = slice(512 * half, 512 * half + 512)
                    out = py[0:rows, 1024 * (t % 2) + 512 * half:1024 * (t % 2) + 512 * half + 512]
                    for k in range(KD):
                        if t == 0 and half == 0:
                            pe.wait_ge(w_lo_done, k + 1)
                        mh, ml = mT_hi[t % 2][:, k, 0:rows], mT_lo[t % 2][:, k, 0:rows]
                        for i, (l, r) in enumerate([(mh, w_hi[:, k, cols]), (mh, w_lo[:, k, cols]),
                                                    (ml, w_hi[:, k, cols])]):
                            mm = nc.tensor.matmul(out, l, r, start=(k == 0 and i == 0), stop=(k == KD - 1 and i == 2))
                mm.then_inc(product, 1)

        @block.scalar
        def _(act):
            def mix_hi(t):
                _, r0, rows = TILES[t]
                act.wait_ge(tr_done, t + 1)
                if t >= 2:
                    act.wait_ge(product, t - 1)
                o = 1024 * (t % 2)
                nc.scalar.copy(mT_hi[t % 2][:, :, 0:rows],
                               pt[:, o:o + 1024].rearrange("p (k r) -> p k r", r=P)[:, :, 0:rows]).then_inc(m_hi, 1)

            for k in range(KD):
                if k == 1:
                    mix_hi(0)
                act.wait_ge(w_loaded[k % 4], 16 * (k // 4 + 1))
                nc.scalar.copy(w_hi[:, k, :], w_raw[k % 4][:, :]).then_inc(w_hi_done, 1)
            for t in range(1, NT + 1):
                mix_hi(t)

        @block.gpsimd
        def _(pool):
            norm.power_first()
            for t, r0, rows in TILES:
                norm.root(pool, t, rows)

        @block.vector
        def _(dve):
            def mix_lo(t):
                _, r0, rows = TILES[t]
                dve.wait_ge(m_hi, t + 1)
                o = 1024 * (t % 2)
                nc.vector.tensor_tensor(mT_lo[t % 2][:, :, 0:rows],
                                        pt[:, o:o + 1024].rearrange("p (k r) -> p k r", r=P)[:, :, 0:rows],
                                        f32(mT_hi[t % 2][:, :, 0:rows]), ALU.subtract).then_inc(m_lo, 1)

            def finish(t):
                _, r0, rows = TILES[t]
                y = pre[t % 2][0:rows, :]
                norm.settled(dve, norm.scaled(dve, t, rows, y))
                nc.vector.tensor_tensor(mix[0:rows, t, :], y, shift[0:rows, :], ALU.add).then_inc(h_done, 1)

            for k in range(KD):
                if k == 1:
                    mix_lo(0)
                dve.wait_ge(w_hi_done, k + 1)
                nc.vector.tensor_tensor(w_lo[:, k, :], w_raw[k % 4][:, :], f32(w_hi[:, k, :]), ALU.subtract)\
                    .then_inc(w_lo_done, 1)
            mix_lo(1)
            for t, r0, rows in TILES:
                dve.wait_ge(x_loaded[t % 2], 16 * (t // 2 + 1))
                dve.wait_ge(product, t + 1)
                if t >= 2:
                    dve.wait_ge(h_done, t - 1)
                y = pre[t % 2][0:rows, :]
                nc.vector.scalar_tensor_tensor(y, x_row[t % 2][0:rows, :], ALPHA,
                                               py[0:rows, 1024 * (t % 2):1024 * (t % 2) + D], ALU.mult, ALU.add)\
                    .then_inc(pre_done, 1)
                if t + 2 <= NT:
                    mix_lo(t + 2)
                dve.wait_ge(pre_done, t + 1)
                norm.moments(dve, t, rows, y)
                if t >= 1:
                    finish(t - 1)
            finish(NT)



def ffn(nc, d, c):
    from contextlib import ExitStack
    with ExitStack() as ctx:
        def sem(name):
            return ctx.enter_context(nc.semaphore(name))

        NB = D_FF // (2 * P)
        NU = 2 * (NT + 1)
        tp = Places(nc, c["t_region"], c["rest"])
        h_hi = tp("h_hi", [P, KD, ROWS], F32R)
        h_lo = tp("h_lo", [P, KD, ROWS], F32R)
        sp_ = Places(nc, -(-nc.sbuf_base // 64) * 64, c["t_region"])
        g_raw = sp_("gate_raw", [P, KD, 2 * P], F32)
        u_raw = sp_("up_raw", [P, KD, 2 * P], F32)
        pl = Places(nc, c["after_mix"], c["end"])
        d_raw = pl("down_raw", [P, 2, D], F32)
        w_hi = [pl(f"gu_hi{s}", [P, KD, P], F32R) for s in range(2)]
        w_lo = [pl(f"gu_lo{s}", [P, KD, P], F32R) for s in range(2)]
        d_hi = pl("down_hi", [P, 2, D], F32R)
        d_lo = pl("down_lo", [P, 2, D], F32R)
        a_hi = pl("act_hi", [P, 2, ROWS], F32R)
        a_lo = pl("act_lo", [P, 2, ROWS], F32R)
        gated = pl("gated", [P, ROWS], F32)
        prod = pl("prod", [P, ROWS], F32)
        gain, shift = pl("ln2_gain", [P, D], F32), pl("ln2_shift", [P, D], F32)
        y, ident = c["mix"], c["ident"]
        pg = ctx.enter_context(nc.psum_tensor("gate", [P, 3, 512], F32))
        pu = ctx.enter_context(nc.psum_tensor("up", [P, 3, 512], F32))
        pd = ctx.enter_context(nc.psum_tensor("down", [P, 2, 512], F32))
        hT_banks = [pu[:, 0, :], pu[:, 1, :], pd[:, 0, :], pd[:, 1, :]]

        g_loaded, u_loaded, d_loaded, ln_loaded = sem("g_loaded"), sem("u_loaded"), sem("d_loaded"), sem("ln_loaded")
        h_tr, h_hi_done, h_lo_done, y_ready = sem("h_tr"), sem("h_hi_done"), sem("h_lo_done"), sem("y_ready")
        w_hi_done, w_lo_done, d_hi_done, d_lo_done = (sem("w_hi_done"), sem("w_lo_done"), sem("d_hi_done"),
                                                      sem("d_lo_done"))
        tile_done, silu_done, prod_done = sem("tile_done"), sem("silu_done"), sem("prod_done")
        a_hi_done, a_lo_done, piece_done, added, down_done = (sem("a_hi_done"), sem("a_lo_done"), sem("piece_done"),
                                                              sem("added"), sem("down_done"))
        scaled_done, shifted, y_stored = sem("scaled_done"), sem("shifted"), sem("y_stored")
        norm = Norm(nc, pl, sem, "ln2", gain, shift, ln_loaded)
        block = ctx.enter_context(nc.Block())

        def blocks(engine, body):
            body(0, True, False)
            with engine.Fori(1, NB - 1) as b:
                body(b, False, False)
            body(NB - 1, False, True)

        @block.sync
        def _(sp):
            def body(b, first, last):
                if not first:
                    sp.wait_ge(w_lo_done, 4 * b - 1)
                sp.dma_start(g_raw[:, :, :], d["w_gate"][:, bass.ds(b * 256, 256)].rearrange(
                    "(k p) n -> p k n", p=P)).then_inc(g_loaded, 16)
                if not first:
                    sp.wait_ge(w_lo_done, 4 * b)
                sp.dma_start(u_raw[:, :, :], d["w_up"][:, bass.ds(b * 256, 256)].rearrange(
                    "(k p) n -> p k n", p=P)).then_inc(u_loaded, 16)
                if not first:
                    sp.wait_ge(d_lo_done, b)
                sp.dma_start(d_raw[:, :, :], d["w_down"][bass.ds(b * 256, 256), :].rearrange(
                    "(f p) n -> p f n", p=P)).then_inc(d_loaded, 16)

            blocks(sp, body)
            sp.dma_start(gain[:, :], d["ln2_g"].partition_broadcast(P)).then_inc(ln_loaded, 16)
            sp.dma_start(shift[:, :], d["ln2_b"].partition_broadcast(P)).then_inc(ln_loaded, 16)
            for t, r0, rows in TILES:
                sp.wait_ge(shifted, t + 1)
                sp.dma_start(d["y"][r0:r0 + rows, :], y[0:rows, t, :]).then_inc(y_stored, 16)
            sp.wait_ge(y_stored, 16 * (NT + 1))

        @block.tensor
        def _(pe):
            def chunk(bank, slot, ch, ks):
                rows = slice(ch * TC, (ch + 1) * TC)
                for k in ks:
                    wh, wl = w_hi[slot][:, k, :], w_lo[slot][:, k, :]
                    for i, (l, r) in enumerate([(wh, h_hi[:, k, rows]), (wh, h_lo[:, k, rows]),
                                                (wl, h_hi[:, k, rows])]):
                        mm = nc.tensor.matmul(bank[:, ch, 0:TC], l, r, start=(k == 0 and i == 0),
                                              stop=(k == KD - 1 and i == 2))
                return mm

            def tile(bank, w, slot):
                pe.wait_ge(w_lo_done, w + 1)
                for ch in range(NCH):
                    mm = chunk(bank, slot, ch, range(KD))
                mm.then_inc(tile_done, 1)

            early = {6 * ch + 8 + i: (ch, range(2 * i, 2 * i + 2)) for ch in range(NCH - 1) for i in range(KD // 2)}
            for q in range(2 * (NT + 1)):
                t, half = q // 2, q % 2
                rows = TILES[t][2]
                if q >= 4:
                    pe.wait_ge(h_lo_done, q - 3)
                for j in range(4):
                    k = 4 * half + j
                    mm = nc.tensor.transpose(hT_banks[q % 4][:, j * P:j * P + rows], y[0:rows, t, k * P:(k + 1) * P],
                                             ident[0:rows, 0:rows])
                mm.then_inc(h_tr, 1)
                if q in early:
                    ch, ks = early[q]
                    if ks[0] == 0:
                        pe.wait_ge(w_lo_done, 1)
                        pe.wait_ge(h_lo_done, 6 * ch + 6)
                    chunk(pg, 0, ch, ks)
            pe.wait_ge(h_lo_done, 2 * (NT + 1))
            chunk(pg, 0, NCH - 1, range(KD)).then_inc(tile_done, 1)

            def down(b, first):
                pe.wait_ge(a_lo_done, 2 * b + 2)
                pe.wait_ge(d_lo_done, b + 1)
                for i in range(NU):
                    t, half = i // 2, i % 2
                    _, r0, rows = TILES[t]
                    if not first or i >= 2:
                        pe.wait_ge(added, b * NU + i - 1)
                    n = 0
                    for f in range(2):
                        ah, al = a_hi[:, f, r0:r0 + rows], a_lo[:, f, r0:r0 + rows]
                        cols = slice(512 * half, 512 * half + 512)
                        for l, r in [(ah, d_hi[:, f, cols]), (ah, d_lo[:, f, cols]), (al, d_hi[:, f, cols])]:
                            mm = nc.tensor.matmul(pd[0:rows, i % 2, :], l, r, start=n == 0, stop=n == 5)
                            n += 1
                    mm.then_inc(piece_done, 1)

            def body(b, first, last):
                if not first:
                    pe.wait_ge(prod_done, 2 * b)
                tile(pu, 4 * b + 1, 1)
                pe.wait_ge(silu_done, 2 * b + 1)
                tile(pg, 4 * b + 2, 0)
                pe.wait_ge(prod_done, 2 * b + 1)
                tile(pu, 4 * b + 3, 1)
                if not last:
                    pe.wait_ge(silu_done, 2 * b + 2)
                    tile(pg, 4 * b + 4, 0)
                down(b, first)

            blocks(pe, body)

        def raw_of(i):
            f = i // 2 % 2
            return (g_raw if i % 2 == 0 else u_raw)[:, :, f * P:(f + 1) * P]

        @block.scalar
        def _(act):
            def split(b, i, first):
                loaded, blk = (g_loaded, u_loaded)[i % 2], b + i // 4
                act.wait_ge(loaded, 16 * blk + 16)
                if not first or i >= 2:
                    act.wait_ge(tile_done, 4 * b + i - 1)
                nc.scalar.copy(w_hi[i % 2][:, :, :], raw_of(i)).then_inc(w_hi_done, 1)

            def silu(b, f):
                act.wait_ge(tile_done, 4 * b + 2 * f + 1)
                if f == 1:
                    act.wait_ge(prod_done, 2 * b + 1)
                nc.scalar.activation(gated[:, :].rearrange("p (c r) -> p c r", c=NCH), pg[:, :, 0:TC], ACT.Silu)\
                    .then_inc(silu_done, 1)

            def act_hi(b, f, first):
                act.wait_ge(prod_done, 2 * b + f + 1)
                if not first and f == 0:
                    act.wait_ge(piece_done, b * NU)
                nc.scalar.copy(a_hi[:, f, :], prod[:, :]).then_inc(a_hi_done, 1)

            for q in range(2 * (NT + 1)):
                t, half = q // 2, q % 2
                _, r0, rows = TILES[t]
                if q == 4:
                    split(0, 0, True)
                act.wait_ge(h_tr, q + 1)
                nc.scalar.copy(h_hi[:, 4 * half:4 * half + 4, r0:r0 + rows],
                               hT_banks[q % 4].rearrange("p (a r) -> p a r", r=P)[:, :, 0:rows]).then_inc(h_hi_done, 1)

            def body(b, first, last):
                split(b, 1, first)
                if not first:
                    act.wait_ge(prod_done, 2 * b)
                silu(b, 0)
                split(b, 2, first)
                act.wait_ge(d_loaded, 16 * b + 16)
                if not first:
                    act.wait_ge(piece_done, b * NU)
                nc.scalar.copy(d_hi[:, :, :], d_raw[:, :, :]).then_inc(d_hi_done, 1)
                act_hi(b, 0, first)
                split(b, 3, first)
                silu(b, 1)
                if not last:
                    split(b, 4, first)
                act_hi(b, 1, first)

            blocks(act, body)

        @block.gpsimd
        def _(pool):
            norm.power_first()

            def split(b, i):
                pool.wait_ge(w_hi_done, 4 * b + i + 1)
                nc.gpsimd.tensor_tensor(w_lo[i % 2][:, :, :], raw_of(i), f32(w_hi[i % 2][:, :, :]), ALU.subtract)\
                    .then_inc(w_lo_done, 1)

            split(0, 0)

            def body(b, first, last):
                split(b, 1)
                split(b, 2)
                pool.wait_ge(d_hi_done, b + 1)
                nc.gpsimd.tensor_tensor(d_lo[:, :, :], d_raw[:, :, :], f32(d_hi[:, :, :]), ALU.subtract)\
                    .then_inc(d_lo_done, 1)
                split(b, 3)
                if not last:
                    split(b, 4)

            blocks(pool, body)

            def shift_rows(t):
                rows = TILES[t][2]
                pool.wait_ge(scaled_done, t + 1)
                nc.gpsimd.tensor_tensor(y[0:rows, t, :], y[0:rows, t, :], shift[0:rows, :], ALU.add)\
                    .then_inc(shifted, 1)

            for t, r0, rows in TILES:
                norm.root(pool, t, rows)
                if t >= 1:
                    shift_rows(t - 1)
            shift_rows(NT)

        @block.vector
        def _(dve):
            for q in range(2 * (NT + 1)):
                t, half = q // 2, q % 2
                _, r0, rows = TILES[t]
                dve.wait_ge(h_hi_done, q + 1)
                nc.vector.tensor_tensor(h_lo[:, 4 * half:4 * half + 4, r0:r0 + rows],
                                        hT_banks[q % 4].rearrange("p (a r) -> p a r", r=P)[:, :, 0:rows],
                                        f32(h_hi[:, 4 * half:4 * half + 4, r0:r0 + rows]), ALU.subtract)\
                    .then_inc(h_lo_done, 1)
                if half == 1:
                    nc.vector.tensor_scalar(y[0:rows, t, :], y[0:rows, t, :], ALPHA, None, ALU.mult)\
                        .then_inc(y_ready, 1)
            dve.wait_ge(y_ready, NT + 1)

            def body(b, first, last):
                for f in range(2):
                    dve.wait_ge(silu_done, 2 * b + f + 1)
                    dve.wait_ge(tile_done, 4 * b + 2 * f + 2)
                    if not first or f >= 1:
                        dve.wait_ge(a_lo_done, 2 * b + f)
                    nc.vector.tensor_tensor(prod[:, :].rearrange("p (c r) -> p c r", c=NCH),
                                            gated[:, :].rearrange("p (c r) -> p c r", c=NCH), pu[:, :, 0:TC], ALU.mult)\
                        .then_inc(prod_done, 1)
                    dve.wait_ge(a_hi_done, 2 * b + f + 1)
                    nc.vector.tensor_tensor(a_lo[:, f, :], prod[:, :], f32(a_hi[:, f, :]), ALU.subtract)\
                        .then_inc(a_lo_done, 1)

                def scale_rows(t):
                    rows = TILES[t][2]
                    norm.scaled(dve, t, rows, y[0:rows, t, :]).then_inc(scaled_done, 1)

                for i in range(NU):
                    t, half = i // 2, i % 2
                    rows = TILES[t][2]
                    o = y[0:rows, t, 512 * half:512 * half + 512]
                    dve.wait_ge(piece_done, b * NU + i + 1)
                    nc.vector.tensor_tensor(o, o, pd[0:rows, i % 2, :], ALU.add).then_inc(added, 1)
                    if last and half == 1:
                        dve.wait_ge(added, b * NU + i + 1)
                        norm.moments(dve, t, rows, y[0:rows, t, :])
                        if t >= 1:
                            scale_rows(t - 1)
                if last:
                    scale_rows(NT)

            blocks(dve, body)


_OUTS = {"y": (ROWS, D), "fkT": (FOX_H * HD, ROWS), "fv": (ROWS, FOX_H * HD), "logf": (ROWS, FOX_H),
         "dk": (ROWS, KV_H * HD), "dv": (ROWS, KV_H * HD), "ik": (ROWS, HD)}
_SCRATCH = {"dq": (ROWS, DSA_H * HD), "negc": (FOX_H, SEQ), "bias_s": (FOX_H, KEYS_S)}


def kernel(**inputs):
    import numpy as np
    import concourse.bacc as bacc
    from concourse.bass_utils import run_bass_kernel_spmd as run

    i = {k: np.asarray(v) for k, v in inputs.items()}
    x = np.concatenate([i["x_prompt"][0], i["x_sample"][0]], 0)
    inv = np.float32(5e5) ** (-np.arange(HALF, dtype=np.float32) * np.float32(2.0) / np.float32(ROT))
    ang = np.zeros(((NT + 1) * P, HALF), np.float32)
    ang[:ROWS] = np.arange(ROWS, dtype=np.float32)[:, None] * inv[None, :].astype(np.float32)
    tiled = lambda a: np.ascontiguousarray(a.astype(np.float32).reshape(NT + 1, P, HALF).transpose(1, 0, 2))
    arrays = {
        "x": x, "xT": x.T, "cos": tiled(np.cos(ang)), "sin": tiled(np.sin(ang)),
        "w_in": i["w_in"][0], "b_forget": i["b_forget"][0], "w_out": i["w_out"][0],
        "ln1_g": i["ln1_g"][0], "ln1_b": i["ln1_b"][0], "ln2_g": i["ln2_g"][0], "ln2_b": i["ln2_b"][0],
        "w_gate": i["w_gate"][0], "w_up": i["w_up"][0], "w_down": i["w_down"][0],
        "past_fkT": i["cache_fox_k"][0, 0].reshape(PAST, -1).T, "past_fv": i["cache_fox_v"][0, 0].reshape(PAST, -1),
        "past_logfT": i["cache_fox_logf"][0, 0].T, "past_dkT": i["cache_dsa_k"][0, 0].reshape(PAST, -1).T,
        "past_dv": i["cache_dsa_v"][0, 0].reshape(PAST, -1), "past_ikT": i["cache_idx_k"][0, 0].T,
    }
    arrays = {k: np.ascontiguousarray(v) for k, v in arrays.items()}
    nc = bacc.Bacc("TRN2", target_bir_lowering=False, num_devices=1)
    d = {k: nc.dram_tensor("in_" + k, v.shape, mybir.dt.from_np(v.dtype), kind="ExternalInput").ap()
         for k, v in arrays.items()}
    for k, shape in _OUTS.items():
        d[k] = nc.dram_tensor("out_" + k, shape, F32, kind="ExternalOutput").ap()
    for k, shape in _SCRATCH.items():
        d[k] = nc.dram_tensor("scratch_" + k, shape, F32, kind="Internal").ap()
    build(nc, d)
    r = run(nc, [{"in_" + k: v for k, v in arrays.items()}], core_ids=[0]).results[0]
    y, fkT, fv, logf, dk, dv, ik = (r["out_" + k] for k in _OUTS)
    fk = fkT.T

    def states(s):
        n = s.stop - s.start
        return (fk[s].reshape(1, 1, n, FOX_H, HD), fv[s].reshape(1, 1, n, FOX_H, HD), logf[s].reshape(1, 1, n, FOX_H),
                dk[s].reshape(1, 1, n, KV_H, HD), dv[s].reshape(1, 1, n, KV_H, HD), ik[s].reshape(1, 1, n, HD))

    p, s = slice(0, SEQ), slice(SEQ, ROWS)
    return (y[p][None], y[s][None], *states(p), *states(s))
```
